# Optimizing a Trainium2 kernel written in Bass

```python
import math
import jax, jax.numpy as jnp
from jax import lax
import numpy as np

D_MODEL = 1024
BATCH = 1
SEQ = 256
DEPTH = 2

GRID_W = 64
CTX_LEN = 256
A_WIDTH = D_MODEL // 4
A_GROUPS = 4
A_GDIM = A_WIDTH // A_GROUPS
CHUNK = 128
B_HEAD_DIM = 64
B_HEADS = (D_MODEL // 2) // B_HEAD_DIM
B_KV_HEADS = B_HEADS // 4
B_WIDTH = B_HEADS * B_HEAD_DIM
WINDOW = 128
BLOCK = 128
C_V_DIM = 64
C_QK_DIM = C_V_DIM // 2
C_HEADS = (D_MODEL // 4) // C_V_DIM
C_WIDTH = C_HEADS * C_V_DIM
Q_BLOCK = 128
MIX_WIDTH = A_WIDTH + B_WIDTH + C_WIDTH
PROJ_SIZES = (2 * A_WIDTH, B_WIDTH, B_KV_HEADS * B_HEAD_DIM, B_KV_HEADS * B_HEAD_DIM,
              C_HEADS * 2 * C_QK_DIM, C_HEADS * 2 * C_QK_DIM, C_WIDTH)
PROJ_WIDTH = sum(PROJ_SIZES)
D_FF = 256 * ((8 * D_MODEL // 3 + 255) // 256)
CONV_W = 3
ROPE_BASE = 10000.0
EPS = 1e-6


def rms_norm(x, gain=None):
    xf = x.astype(jnp.float32)
    y = xf * lax.rsqrt(jnp.mean(xf * xf, axis=-1, keepdims=True) + EPS)
    if gain is not None:
        y = y * gain.astype(jnp.float32)
    return y.astype(x.dtype)

def modulation(cond, w_ada, b_ada):
    m = jax.nn.silu(cond) @ w_ada + b_ada
    return [t[..., None, :] for t in jnp.split(m, 6, axis=-1)]

def modulate(h, shift, scale):
    return h * (1 + scale) + shift

def split_proj(z):
    idx = np.cumsum(np.array(PROJ_SIZES))[:-1].tolist()
    return jnp.split(z, idx, axis=-1)

def axial_rope(n_tokens, head_dim):
    rows = n_tokens // GRID_W
    row = jnp.repeat(jnp.arange(rows, dtype=jnp.float32), GRID_W)
    col = jnp.tile(jnp.arange(GRID_W, dtype=jnp.float32), rows)
    n_freq = head_dim // 4
    inv_freq = ROPE_BASE ** (-jnp.arange(n_freq, dtype=jnp.float32) / n_freq)
    ang = jnp.stack([row[:, None] * inv_freq, col[:, None] * inv_freq], axis=1)
    return jnp.cos(ang), jnp.sin(ang)

def apply_rope(x, cos, sin):
    b, l, h, d = x.shape
    xr = x.reshape(b, l, h, 2, 2, d // 4).astype(jnp.float32)
    x1, x2 = xr[..., 0, :], xr[..., 1, :]
    c = cos[None, :, None]
    s = sin[None, :, None]
    out = jnp.stack([x1 * c - x2 * s, x2 * c + x1 * s], axis=-2)
    return out.reshape(b, l, h, d).astype(x.dtype)

def rope_maps(t, cos, sin):
    b, l, h, m, d = t.shape
    return apply_rope(t.reshape(b, l, h * m, d), cos, sin).reshape(b, l, h, m, d)

def chunk_gmlp(z, w_s, b_s):
    b, l, _ = z.shape
    z = jax.nn.gelu(z)
    u, v = jnp.split(z, 2, axis=-1)
    v = rms_norm(v.reshape(b, l // CHUNK, CHUNK, A_GROUPS, A_GDIM))
    mixed = jnp.einsum('gpq,bnqgc->bnpgc', w_s, v) + b_s.T[None, None, :, :, None]
    return u * mixed.reshape(b, l, A_WIDTH)

def window_attn_latent(q, k, v, k_ctx, v_ctx, sink):
    b, l, hq, d = q.shape
    hkv = k.shape[2]
    g = hq // hkv
    nb = l // BLOCK
    lc = k_ctx.shape[1]
    scale = d ** -0.5
    qb = q.reshape(b, nb, BLOCK, hkv, g, d)

    def band(t):
        tb = jnp.pad(t.reshape(b, nb, BLOCK, hkv, d), ((0, 0), (1, 1), (0, 0), (0, 0), (0, 0)))
        return jnp.concatenate([tb[:, :-2], tb[:, 1:-1], tb[:, 2:]], axis=2)

    kb, vb = band(k), band(v)
    s_win = jnp.einsum('bnqhgd,bnkhd->bnhgqk', qb, kb).astype(jnp.float32) * scale
    qpos = jnp.arange(nb)[:, None, None] * BLOCK + jnp.arange(BLOCK)[None, :, None]
    kpos = (jnp.arange(nb)[:, None, None] - 1) * BLOCK + jnp.arange(3 * BLOCK)[None, None, :]
    valid = (kpos >= 0) & (kpos < l) & (jnp.abs(qpos - kpos) <= WINDOW)
    s_win = jnp.where(valid[None, :, None, None], s_win, -jnp.inf)
    s_ctx = jnp.einsum('bnqhgd,bkhd->bnhgqk', qb, k_ctx).astype(jnp.float32) * scale
    s_sink = jnp.broadcast_to(sink.astype(jnp.float32).reshape(hkv, g)[None, None, :, :, None, None],
                              s_win.shape[:-1] + (1,))
    p = jax.nn.softmax(jnp.concatenate([s_win, s_ctx, s_sink], axis=-1), axis=-1)
    kw = 3 * BLOCK
    p_win = p[..., :kw].astype(v.dtype)
    p_ctx = p[..., kw:kw + lc].astype(v.dtype)
    o = (jnp.einsum('bnhgqk,bnkhd->bnqhgd', p_win, vb)
         + jnp.einsum('bnhgqk,bkhd->bnqhgd', p_ctx, v_ctx))
    return o.reshape(b, l, hq * d)

def sink_attn_ctx(q, k, v, sink):
    b, lc, hq, d = q.shape
    hkv = k.shape[2]
    g = hq // hkv
    qg = q.reshape(b, lc, hkv, g, d)
    s = jnp.einsum('bqhgd,bkhd->bhgqk', qg, k).astype(jnp.float32) * d ** -0.5
    s_sink = jnp.broadcast_to(sink.astype(jnp.float32).reshape(1, hkv, g, 1, 1), (b, hkv, g, lc, 1))
    p = jax.nn.softmax(jnp.concatenate([s, s_sink], axis=-1), axis=-1)[..., :lc]
    o = jnp.einsum('bhgqk,bkhd->bqhgd', p.astype(v.dtype), v)
    return o.reshape(b, lc, hq * d)

def diff_lambda(lam_params, lam_init):
    lp = lam_params.astype(jnp.float32)
    return jnp.exp(jnp.sum(lp[0] * lp[1])) - jnp.exp(jnp.sum(lp[2] * lp[3])) + lam_init

def diff_attn_block(q, k, v, lam):
    s = jnp.einsum('bqhmd,bkhmd->bhmqk', q, k).astype(jnp.float32) * q.shape[-1] ** -0.5
    p = jax.nn.softmax(s, axis=-1)
    pd = p[:, :, 0] - lam * p[:, :, 1]
    return jnp.einsum('bhqk,bkhd->bqhd', pd.astype(v.dtype), v)

def diff_attn_latent(q, k, v, k_ctx, v_ctx, lam):
    b, l, h, _, dq = q.shape
    k_all = jnp.concatenate([k, k_ctx], axis=1)
    v_all = jnp.concatenate([v, v_ctx], axis=1)
    qb = jnp.moveaxis(q.reshape(b, l // Q_BLOCK, Q_BLOCK, h, 2, dq), 1, 0)
    o = lax.map(lambda qblk: diff_attn_block(qblk, k_all, v_all, lam), qb)
    return jnp.moveaxis(o, 0, 1).reshape(b, l, h, -1)

def conv_ffn(h, w_up, conv_w, conv_b, w_down):
    a = h @ w_up
    a = lax.conv_general_dilated(a, conv_w, window_strides=(1,), padding=((CONV_W // 2, CONV_W // 2),),
                                 dimension_numbers=('NWC', 'WIO', 'NWC'),
                                 feature_group_count=a.shape[-1]) + conv_b
    gate, val = jnp.split(a, 2, axis=-1)
    return (jax.nn.silu(gate) * val) @ w_down

def first_inputs(seed: int = 0) -> dict:
    key = jax.random.key(seed)
    ks = jax.random.split(key, 24)
    nrm = jax.random.normal
    f32 = jnp.float32
    L = DEPTH
    D = D_MODEL
    return {
        'x': nrm(ks[0], (BATCH, SEQ, D), f32),
        'c': nrm(ks[1], (BATCH, D), f32),
        'ctx': nrm(ks[2], (BATCH, CTX_LEN, D), f32),
        'c_ctx': nrm(ks[3], (D,), f32),
        'w_ada': nrm(ks[4], (L, D, 6 * D), f32) * (0.25 * D ** -0.5),
        'b_ada': nrm(ks[5], (L, 6 * D), f32) * 0.01,
        'norm1_g': 1.0 + 0.02 * nrm(ks[6], (L, D), f32),
        'norm2_g': 1.0 + 0.02 * nrm(ks[7], (L, D), f32),
        'w_in': nrm(ks[8], (L, D, PROJ_WIDTH), f32) * D ** -0.5,
        'a_ws': nrm(ks[9], (L, A_GROUPS, CHUNK, CHUNK), f32) * CHUNK ** -0.5,
        'a_bs': 1.0 + 0.02 * nrm(ks[10], (L, A_GROUPS, CHUNK), f32),
        'b_qnorm': 1.0 + 0.02 * nrm(ks[11], (L, B_HEAD_DIM), f32),
        'b_knorm': 1.0 + 0.02 * nrm(ks[12], (L, B_HEAD_DIM), f32),
        'b_sink': 0.5 * nrm(ks[13], (L, B_HEADS), f32),
        'c_qnorm': 1.0 + 0.02 * nrm(ks[14], (L, C_QK_DIM), f32),
        'c_knorm': 1.0 + 0.02 * nrm(ks[15], (L, C_QK_DIM), f32),
        'c_lam': 0.1 * nrm(ks[16], (L, 4, C_QK_DIM), f32),
        'c_subln': 1.0 + 0.02 * nrm(ks[17], (L, C_V_DIM), f32),
        'w_out': nrm(ks[18], (L, MIX_WIDTH, D), f32) * MIX_WIDTH ** -0.5,
        'w_up': nrm(ks[19], (L, D, 2 * D_FF), f32) * D ** -0.5,
        'conv_w': nrm(ks[20], (L, CONV_W, 1, 2 * D_FF), f32) * CONV_W ** -0.5,
        'conv_b': 0.01 * nrm(ks[21], (L, 2 * D_FF), f32),
        'w_down': nrm(ks[22], (L, D_FF, D), f32) * D_FF ** -0.5,
    }

def first_block(x, c, ctx, c_ctx, w_ada, b_ada, norm1_g, norm2_g, w_in, a_ws, a_bs,
              b_qnorm, b_knorm, b_sink, c_qnorm, c_knorm, c_lam, c_subln,
              w_out, w_up, conv_w, conv_b, w_down):
    b, l, _ = x.shape
    lc = ctx.shape[1]
    cos_b, sin_b = axial_rope(l, B_HEAD_DIM)
    cos_c, sin_c = axial_rope(l, C_QK_DIM)
    for i in range(DEPTH):
        last = i == DEPTH - 1
        lam_init = 0.8 - 0.6 * math.exp(-0.3 * i)
        sh1, sc1, g1, sh2, sc2, g2 = modulation(c, w_ada[i], b_ada[i])
        csh1, csc1, cg1, csh2, csc2, cg2 = modulation(c_ctx, w_ada[i], b_ada[i])

        h = modulate(rms_norm(x, norm1_g[i]), sh1, sc1)
        hc = modulate(rms_norm(ctx, norm1_g[i]), csh1, csc1)
        a_z, bq, bk, bv, cq, ck, cv = split_proj(h @ w_in[i])
        a_zc, bqc, bkc, bvc, cqc, ckc, cvc = split_proj(hc @ w_in[i])

        k_bc = rms_norm(bkc.reshape(b, lc, B_KV_HEADS, B_HEAD_DIM), b_knorm[i])
        v_bc = bvc.reshape(b, lc, B_KV_HEADS, B_HEAD_DIM)
        k_cc = rms_norm(ckc.reshape(b, lc, C_HEADS, 2, C_QK_DIM), c_knorm[i])
        v_cc = cvc.reshape(b, lc, C_HEADS, C_V_DIM)
        lam = diff_lambda(c_lam[i], lam_init)

        out_a = chunk_gmlp(a_z, a_ws[i], a_bs[i])
        q_b = apply_rope(rms_norm(bq.reshape(b, l, B_HEADS, B_HEAD_DIM), b_qnorm[i]), cos_b, sin_b)
        k_b = apply_rope(rms_norm(bk.reshape(b, l, B_KV_HEADS, B_HEAD_DIM), b_knorm[i]), cos_b, sin_b)
        v_b = bv.reshape(b, l, B_KV_HEADS, B_HEAD_DIM)
        out_b = window_attn_latent(q_b, k_b, v_b, k_bc, v_bc, b_sink[i])
        q_c = rope_maps(rms_norm(cq.reshape(b, l, C_HEADS, 2, C_QK_DIM), c_qnorm[i]), cos_c, sin_c)
        k_c = rope_maps(rms_norm(ck.reshape(b, l, C_HEADS, 2, C_QK_DIM), c_knorm[i]), cos_c, sin_c)
        v_c = cv.reshape(b, l, C_HEADS, C_V_DIM)
        o_c = diff_attn_latent(q_c, k_c, v_c, k_cc, v_cc, lam)
        out_c = (rms_norm(o_c, c_subln[i]) * (1 - lam_init)).reshape(b, l, C_WIDTH)

        x = x + g1 * (jnp.concatenate([out_a, out_b, out_c], axis=-1) @ w_out[i])
        x = x + g2 * conv_ffn(modulate(rms_norm(x, norm2_g[i]), sh2, sc2),
                              w_up[i], conv_w[i], conv_b[i], w_down[i])

        if not last:
            out_ac = chunk_gmlp(a_zc, a_ws[i], a_bs[i])
            q_bc = rms_norm(bqc.reshape(b, lc, B_HEADS, B_HEAD_DIM), b_qnorm[i])
            out_bc = sink_attn_ctx(q_bc, k_bc, v_bc, b_sink[i])
            q_cc = rms_norm(cqc.reshape(b, lc, C_HEADS, 2, C_QK_DIM), c_qnorm[i])
            o_cc = diff_attn_block(q_cc, k_cc, v_cc, lam)
            out_cc = (rms_norm(o_cc, c_subln[i]) * (1 - lam_init)).reshape(b, lc, C_WIDTH)
            ctx = ctx + cg1 * (jnp.concatenate([out_ac, out_bc, out_cc], axis=-1) @ w_out[i])
            ctx = ctx + cg2 * conv_ffn(modulate(rms_norm(ctx, norm2_g[i]), csh2, csc2),
                                       w_up[i], conv_w[i], conv_b[i], w_down[i])
    return x


CHUNK_2 = 64
LEFT_CHUNKS = 8
BAND_CHUNKS = LEFT_CHUNKS + 1
N_HEADS = 16
HEAD_DIM = D_MODEL // N_HEADS
REL_CLIP = 128
LRU_WIDTH = ((4 * D_MODEL // 3 + 127) // 128) * 128
N_LRU_BLOCKS = 16
LRU_BLOCK = LRU_WIDTH // N_LRU_BLOCKS
LRU_C = 8.0
CONV_WIDTH = 4
D_FF_2 = 4 * D_MODEL
N_A_LAYERS = DEPTH // 2
N_B_LAYERS = DEPTH - N_A_LAYERS


def rms_norm_2(x, g):
    xf = x.astype(jnp.float32)
    y = xf * lax.rsqrt(jnp.mean(xf * xf, axis=-1, keepdims=True) + EPS)
    return (y * g.astype(jnp.float32)).astype(x.dtype)

def modulate_2(x, shift, scale):
    return x * (1 + scale[:, None, :]) + shift[:, None, :]

def causal_depthwise_conv(x, w, b):
    y = lax.conv_general_dilated(
        x, w[:, None, :].astype(x.dtype), window_strides=(1,),
        padding=[(CONV_WIDTH - 1, 0)],
        dimension_numbers=("NWC", "WIO", "NWC"),
        feature_group_count=x.shape[-1])
    return y + b

def rg_lru(x, w_a, b_a, w_x, b_x, lam):
    bsz, s, w = x.shape
    xb = x.reshape(bsz, s, N_LRU_BLOCKS, LRU_BLOCK)
    r = jax.nn.sigmoid(jnp.einsum("bsnd,nde->bsne", xb, w_a).reshape(bsz, s, w) + b_a)
    i = jax.nn.sigmoid(jnp.einsum("bsnd,nde->bsne", xb, w_x).reshape(bsz, s, w) + b_x)
    log_a = (-LRU_C * r.astype(jnp.float32)) * jax.nn.softplus(-lam.astype(jnp.float32))
    a = jnp.exp(log_a)
    mult = jnp.sqrt(-jnp.expm1(2.0 * log_a))
    u = mult * (i * x).astype(jnp.float32)

    def combine(left, right):
        a_l, b_l = left
        a_r, b_r = right
        return a_r * a_l, a_r * b_l + b_r

    _, h = lax.associative_scan(combine, (a, u), axis=1)
    return h.astype(x.dtype)

def recurrent_mixer(hn, w_in, conv_w, conv_b, gate_a_w, gate_a_b, gate_x_w, gate_x_b, lam, w_out):
    z = hn @ w_in
    gate, xr = jnp.split(z, 2, axis=-1)
    xr = causal_depthwise_conv(xr, conv_w, conv_b)
    y = rg_lru(xr, gate_a_w, gate_a_b, gate_x_w, gate_x_b, lam)
    return (y * jax.nn.gelu(gate)) @ w_out

def shared_kv(h, c_act, kv_norm_g, kv_ada_w, kv_ada_b, kv_w, k_norm_g):
    bsz, s, _ = h.shape
    shift, scale = jnp.split(c_act @ kv_ada_w + kv_ada_b, 2, axis=-1)
    hn = modulate_2(rms_norm_2(h, kv_norm_g), shift, scale)
    k, v = jnp.split(hn @ kv_w, 2, axis=-1)
    k = rms_norm_2(k.reshape(bsz, s, N_HEADS, HEAD_DIM), k_norm_g)
    v = v.reshape(bsz, s, N_HEADS, HEAD_DIM)
    pad = ((0, 0), (LEFT_CHUNKS * CHUNK_2, 0), (0, 0), (0, 0))
    return jnp.pad(k, pad), jnp.pad(v, pad)

def chunk_attention(hn, w_q, q_norm_g, rel_bias, w_o, k_pad, v_pad):
    bsz, s, d = hn.shape
    n_chunks = s // CHUNK_2
    band = BAND_CHUNKS * CHUNK_2
    left = LEFT_CHUNKS * CHUNK_2
    q = rms_norm_2((hn @ w_q).reshape(bsz, s, N_HEADS, HEAD_DIM), q_norm_g)
    q_chunks = q.reshape(bsz, n_chunks, CHUNK_2, N_HEADS, HEAD_DIM).transpose(1, 0, 2, 3, 4)
    rel = jnp.arange(CHUNK_2)[:, None] - (jnp.arange(band)[None, :] - left)
    rel_idx = jnp.clip(rel, -REL_CLIP, REL_CLIP) + REL_CLIP
    bias = rel_bias[:, rel_idx].astype(jnp.float32)
    scale = HEAD_DIM ** -0.5

    def one_chunk(args):
        qc, ci = args
        start = ci * CHUNK_2
        kc = lax.dynamic_slice_in_dim(k_pad, start, band, axis=1)
        vc = lax.dynamic_slice_in_dim(v_pad, start, band, axis=1)
        sc = jnp.einsum("bqhd,bkhd->bhqk", qc, kc,
                        preferred_element_type=jnp.float32) * scale + bias
        valid = (start - left + jnp.arange(band)) >= 0
        sc = jnp.where(valid[None, None, None, :], sc, -1e30)
        p = jax.nn.softmax(sc, axis=-1).astype(vc.dtype)
        return jnp.einsum("bhqk,bkhd->bqhd", p, vc)

    out = lax.map(one_chunk, (q_chunks, jnp.arange(n_chunks)))
    out = out.transpose(1, 0, 2, 3, 4).reshape(bsz, s, d)
    return out @ w_o

def sqrelu_mlp(hn, w1, w2):
    return jnp.square(jax.nn.relu(hn @ w1)) @ w2

def second_inputs(seed: int = 0) -> dict:
    key = jax.random.key(seed)
    ks = jax.random.split(key, 32)
    f32 = jnp.float32
    D, W = D_MODEL, LRU_WIDTH

    def nrm(k, shape, fan_in):
        return jax.random.normal(k, shape, f32) * (fan_in ** -0.5)

    u = jax.random.uniform(ks[10], (N_A_LAYERS, W), f32, 0.9, 0.999)
    a0 = u ** (1.0 / LRU_C)
    lru_lambda = jnp.log(a0) - jnp.log1p(-a0)
    return {
        "x": jax.random.normal(ks[0], (BATCH, SEQ, D), f32),
        "c": jax.random.normal(ks[1], (BATCH, D), f32),
        "ada_w": nrm(ks[2], (DEPTH, D, 6 * D), D),
        "ada_b": 0.02 * jax.random.normal(ks[3], (DEPTH, 6 * D), f32),
        "norm1_g": 1.0 + 0.05 * jax.random.normal(ks[4], (DEPTH, D), f32),
        "norm2_g": 1.0 + 0.05 * jax.random.normal(ks[5], (DEPTH, D), f32),
        "mlp_w1": nrm(ks[6], (DEPTH, D, D_FF_2), D),
        "mlp_w2": nrm(ks[7], (DEPTH, D_FF_2, D), D_FF_2),
        "lru_w_in": nrm(ks[8], (N_A_LAYERS, D, 2 * W), D),
        "lru_conv_w": nrm(ks[9], (N_A_LAYERS, CONV_WIDTH, W), CONV_WIDTH),
        "lru_conv_b": 0.02 * jax.random.normal(ks[11], (N_A_LAYERS, W), f32),
        "lru_gate_a_w": nrm(ks[12], (N_A_LAYERS, N_LRU_BLOCKS, LRU_BLOCK, LRU_BLOCK), LRU_BLOCK),
        "lru_gate_a_b": 0.02 * jax.random.normal(ks[13], (N_A_LAYERS, W), f32),
        "lru_gate_x_w": nrm(ks[14], (N_A_LAYERS, N_LRU_BLOCKS, LRU_BLOCK, LRU_BLOCK), LRU_BLOCK),
        "lru_gate_x_b": 0.02 * jax.random.normal(ks[15], (N_A_LAYERS, W), f32),
        "lru_lambda": lru_lambda,
        "lru_w_out": nrm(ks[16], (N_A_LAYERS, W, D), W),
        "kv_norm_g": 1.0 + 0.05 * jax.random.normal(ks[17], (D,), f32),
        "kv_ada_w": nrm(ks[18], (D, 2 * D), D),
        "kv_ada_b": 0.02 * jax.random.normal(ks[19], (2 * D,), f32),
        "kv_w": nrm(ks[20], (D, 2 * D), D),
        "k_norm_g": 1.0 + 0.05 * jax.random.normal(ks[21], (HEAD_DIM,), f32),
        "attn_w_q": nrm(ks[22], (N_B_LAYERS, D, D), D),
        "q_norm_g": 1.0 + 0.05 * jax.random.normal(ks[23], (N_B_LAYERS, HEAD_DIM), f32),
        "rel_bias": 0.5 * jax.random.normal(ks[24], (N_B_LAYERS, N_HEADS, 2 * REL_CLIP + 1), f32),
        "attn_w_o": nrm(ks[25], (N_B_LAYERS, D, D), D),
    }

def second_block(x, c, ada_w, ada_b, norm1_g, norm2_g, mlp_w1, mlp_w2,
              lru_w_in, lru_conv_w, lru_conv_b, lru_gate_a_w, lru_gate_a_b,
              lru_gate_x_w, lru_gate_x_b, lru_lambda, lru_w_out,
              kv_norm_g, kv_ada_w, kv_ada_b, kv_w, k_norm_g,
              attn_w_q, q_norm_g, rel_bias, attn_w_o):
    c_act = jax.nn.silu(c)
    h = x
    k_pad = None
    v_pad = None
    for layer in range(DEPTH):
        mod = c_act @ ada_w[layer] + ada_b[layer]
        sh1, sc1, g1, sh2, sc2, g2 = jnp.split(mod, 6, axis=-1)
        hn = modulate_2(rms_norm_2(h, norm1_g[layer]), sh1, sc1)
        if layer < N_A_LAYERS:
            y = recurrent_mixer(hn, lru_w_in[layer], lru_conv_w[layer], lru_conv_b[layer],
                                lru_gate_a_w[layer], lru_gate_a_b[layer],
                                lru_gate_x_w[layer], lru_gate_x_b[layer],
                                lru_lambda[layer], lru_w_out[layer])
        else:
            j = layer - N_A_LAYERS
            y = chunk_attention(hn, attn_w_q[j], q_norm_g[j], rel_bias[j], attn_w_o[j],
                                k_pad, v_pad)
        h = h + g1[:, None, :] * y
        hn = modulate_2(rms_norm_2(h, norm2_g[layer]), sh2, sc2)
        h = h + g2[:, None, :] * sqrelu_mlp(hn, mlp_w1[layer], mlp_w2[layer])
        if layer == N_A_LAYERS - 1:
            k_pad, v_pad = shared_kv(h, c_act, kv_norm_g, kv_ada_w, kv_ada_b, kv_w, k_norm_g)
    return h


def setup_inputs(seed=0):
    out = dict(first_inputs(seed))
    for name, value in second_inputs(seed + 1).items():
        if name != "x":
            out[name + "_2"] = value
    return out


def reference(
    x, c, ctx, c_ctx, w_ada, b_ada, norm1_g, norm2_g, w_in, a_ws, a_bs, b_qnorm, b_knorm,
    b_sink, c_qnorm, c_knorm, c_lam, c_subln, w_out, w_up, conv_w, conv_b, w_down, c_2, ada_w_2,
    ada_b_2, norm1_g_2, norm2_g_2, mlp_w1_2, mlp_w2_2, lru_w_in_2, lru_conv_w_2, lru_conv_b_2,
    lru_gate_a_w_2, lru_gate_a_b_2, lru_gate_x_w_2, lru_gate_x_b_2, lru_lambda_2, lru_w_out_2,
    kv_norm_g_2, kv_ada_w_2, kv_ada_b_2, kv_w_2, k_norm_g_2, attn_w_q_2, q_norm_g_2, rel_bias_2,
    attn_w_o_2,
):
    x = first_block(
        x, c, ctx, c_ctx, w_ada, b_ada, norm1_g, norm2_g, w_in, a_ws, a_bs, b_qnorm, b_knorm,
        b_sink, c_qnorm, c_knorm, c_lam, c_subln, w_out, w_up, conv_w, conv_b, w_down,
    )
    return second_block(
        x, c_2, ada_w_2, ada_b_2, norm1_g_2, norm2_g_2, mlp_w1_2, mlp_w2_2, lru_w_in_2,
        lru_conv_w_2, lru_conv_b_2, lru_gate_a_w_2, lru_gate_a_b_2, lru_gate_x_w_2,
        lru_gate_x_b_2, lru_lambda_2, lru_w_out_2, kv_norm_g_2, kv_ada_w_2, kv_ada_b_2, kv_w_2,
        k_norm_g_2, attn_w_q_2, q_norm_g_2, rel_bias_2, attn_w_o_2,
    )


_drawn_inputs = setup_inputs


def setup_inputs(seed=0):
    import zlib

    import numpy as np

    out = dict(_drawn_inputs(seed))
    spreads = {}
    factors = {'b_ada': 3.143,
     'norm1_g': 8.0,
     'norm2_g': 8.0,
     'a_bs': 8.0,
     'b_qnorm': 8.0,
     'b_knorm': 8.0,
     'b_sink': 8.0,
     'c_qnorm': 8.0,
     'c_knorm': 8.0,
     'c_lam': 8.0,
     'c_subln': 8.0,
     'conv_b': 8.0,
     'lru_gate_a_b_2': 45.411,
     'lru_gate_x_b_2': 8.0,
     'kv_norm_g_2': 6.483,
     'kv_ada_b_2': 8.0,
     'k_norm_g_2': 8.0,
     'q_norm_g_2': 8.0,
     'rel_bias_2': 3.048,
     'lru_conv_b_2': 4.896}
    for name, (base, spread) in spreads.items():
        noise = np.random.default_rng([zlib.crc32(name.encode()), seed]).standard_normal(out[name].shape)
        drawn = base * np.exp(spread * noise) if base else spread * noise
        out[name] = __import__('jax').numpy.asarray(drawn.astype(out[name].dtype))
    for name, factor in factors.items():
        out[name] = (out[name] * factor).astype(out[name].dtype)
    return out
```

```python
from contextlib import ExitStack
import math

import numpy as np
import concourse.bass as bass
from concourse import mybir

F32 = mybir.dt.float32
F32R = mybir.dt.float32r
ALU = mybir.AluOpType
ACT = mybir.ActivationFunctionType
AX = mybir.AxisListType.X

P = 128
D = 1024
KD = D // P
SEQ = 256
CTX = 256
FF = 2816
NFF = FF // P
HALF = NFF // 2
LW = 1408
NL = LW // P
LB = 88
FF2 = 4096
EPS = 1e-6
NEG = -1e30
UMAX = 2048
RAW, SPLIT = 4, 3
AUXN = 3
HEADS_B = [0, 4, 1, 5, 2, 6, 3, 7]

ROWS = {}
_n = 0
for _l in range(2):
    for _name, _w in (("bq", 64), ("bk", 64), ("cq", 32), ("ck", 32), ("lam", 128), ("sub", 64), ("sink", 8)):
        ROWS[_name, _l] = (_n, _w)
        _n += _w
for _name in ("k2", "q2"):
    ROWS[_name, 0] = (_n, 64)
    _n += 64
NROW = _n
NVEC = 26
CTXV = 8
FEAT = {}
_n = 0
for _name, _w in (("bada", NVEC * 8), ("norm", 9 * 8), ("cw", 2 * 3 * 44), ("cb", 2 * 44), ("lcw", 4 * NL), ("lcb", NL),
                  ("lba", NL), ("lbx", NL), ("lam", NL), ("c", 24)):
    FEAT[_name] = _n
    _n += _w
NFEAT = _n
CONST = {"ident": 0, "ones": 128, "mask": 256, "cb": 512, "sb": 640, "cc": 768, "sc": 832}
NCONST = 896


def gate_tiles():
    out = []
    for j in range(NL):
        lo = (P * j) // LB * LB
        hi = min(-(-(P * (j + 1)) // LB) * LB, LW)
        out.append([m for m in range(NL) if P * m < hi and P * (m + 1) > lo])
    return out


GATES = gate_tiles()
GATE_UNITS = [list(range(a, min(a + 2, NL))) for a in range(0, NL, 2)]
MODTYPE = ["shift", "scale", "gate", "shift", "scale", "gate"]


def vec_base(stage):
    return {"L0": 0, "L1": 6, "M0": 12, "KV": 18, "M1": 20}[stage]


def make_units():
    u = []

    def add(kind, st, idx, kt, cols, T, **more):
        u.append(dict(kind=kind, st=st, idx=idx, kt=kt, cols=cols, T=T, i=len(u), **more))

    for l in range(2):
        T = 512 if l == 0 else 256
        st = f"L{l}"
        full, own = (4, 4) if l == 0 else (4, 2)
        for n, (name, nt) in enumerate([("bq0", own), ("bq1", own), ("bkv", full), ("cq", own), ("ck", full),
                                        ("cv", full), ("av", own), ("au", own)]):
            add(name, st, n, KD, 256, nt * 128, nt=nt)
        for n in range(4):
            add("out", st, n, KD, 256, T)
        for h in range(2):
            for n in range(HALF):
                add("up", st, h * HALF + n, KD, 256, T)
            for n in range(KD):
                add("down", st, h * KD + n, HALF, 128, T)
    for n in range(NL):
        add("lin", "M0", n, KD, 256, 256)
    for n in range(len(GATE_UNITS)):
        add("lgate", "M0", n, 2 * sum(len(GATES[j]) for j in GATE_UNITS[n]), 128, 256)
    for n in range(KD):
        add("lout", "M0", n, NL, 128, 256)

    def mlp(st):
        for h in range(2):
            for n in range(8):
                add("w1", st, h * 8 + n, KD, 256, 256)
            for n in range(KD):
                add("w2", st, h * KD + n, 16, 128, 256)

    mlp("M0")
    for n in range(8):
        add("k" if n < 4 else "v", "KV", n, KD, 256, 256, nt=2)
    for n in range(4):
        add("q", "M1", n, KD, 256, 256, nt=2)
    for n in range(4):
        add("out", "M1", n, KD, 256, 256)
    mlp("M1")
    return u


UNITS = make_units()
NU = len(UNITS)


def first_of(kind, st):
    return next(u["i"] for u in UNITS if u["kind"] == kind and u["st"] == st)


def make_program():
    prog = [("norm", 0, "L0", 512)]
    n = 1
    for st in ("L0", "L1", "M0", "KV", "M1"):
        for u in UNITS:
            if u["st"] != st:
                continue
            key = (u["kind"], u["idx"])
            if st in ("L0", "L1"):
                if key == ("out", 0):
                    prog.append(("attn", st))
                if key == ("up", 0):
                    prog.append(("norm", 1 + 2 * int(st[1]), st, 512 if st == "L0" else 256))
                if key == ("bq0", 0) and st == "L1":
                    prog.append(("norm", 2, "L1", 512))
            if st == "M0":
                if key == ("lin", 0):
                    prog.append(("norm", 4, "M0", 256))
                if key == ("lgate", 0):
                    prog.append(("lsplit",))
                if key == ("lout", 0):
                    prog.append(("lscan",))
                if key == ("w1", 0):
                    prog.append(("norm", 5, "M0", 256))
            if key == ("k", 0):
                prog.append(("norm", 6, "KV", 256))
            if st == "M1":
                if key == ("q", 0):
                    prog.append(("norm", 7, "M1", 256))
                if key == ("out", 0):
                    prog.append(("attn", "M1"))
                if key == ("w1", 0):
                    prog.append(("norm", 8, "M1", 256))
            prog.append(("unit", u["i"]))
    return prog


PROGRAM = make_program()
FEEDS = {("out", "L0"): 1, ("down", "L0"): 2, ("out", "L1"): 3, ("down", "L1"): 4, ("lout", "M0"): 5,
         ("w2", "M0"): 6, ("out", "M1"): 8}
FIRST_HALF = {"down": KD, "w2": KD}


def fed_norm(u):
    n = FEEDS.get((u["kind"], u["st"]))
    if n is None or u["idx"] < FIRST_HALF.get(u["kind"], 0):
        return None
    return n


def chunks_of(u):
    if u["kind"] == "out":
        return [2 * u["idx"], 2 * u["idx"] + 1]
    return [u["idx"] % KD]


def ada_plan():
    n = [0] * NU
    for i in range(0, 4):
        n[i] = 1
    for i in range(4, 8):
        n[i] = 2
    for i in range(8, 36):
        n[i] = 1
    for i in range(first_of("out", "L1"), first_of("out", "L1") + 24):
        n[i] = 1
    for i in range(first_of("lin", "M0"), first_of("lin", "M0") + 32):
        n[i] = 1
    out, at = [], 8
    for i in range(NU):
        out.append(list(range(at, at + n[i])))
        at += n[i]
    assert at == NVEC * 4
    return out


ADA_AT = ada_plan()
ADA_FIRST = list(range(8))
REDUCE_AT = [[a // 2 for a in (ADA_AT[i - 1] if i else []) if a % 2] for i in range(NU)]


def raw_order():
    order = [("ada", a) for a in ADA_FIRST] + [("w", 0), ("w", 1)]
    for i in range(NU):
        if i + 2 < NU:
            order.append(("w", i + 2))
        order += [("ada", a) for a in ADA_AT[i]]
    return order


RAW_ORDER = raw_order()
RAW_AT = {key: n for n, key in enumerate(RAW_ORDER)}


def attention_tiles(st):
    out = []
    if st == "M1":
        for t in range(2):
            for hg in range(2):
                for s in range(8):
                    h = hg * 8 + s
                    out.append(dict(st=st, t=t, grp=("m", t, hg), slot=s, qc=h // 2, kc=h // 2, base=64 * (h % 2), K=64,
                                    k0=0, nk=128 * (t + 1), h=h, v=[(kt, 64 * h) for kt in range(t + 1)]))
        return out
    for t in range(4 if st == "L0" else 2):
        kts = [0, 1, 2, 3] if t < 2 else [2, 3]
        for s in range(8):
            out.append(dict(st=st, t=t, grp=("b", t), slot=s, qc=s // 2, kc=4, base=64 * (s % 2), K=64, k0=128 * kts[0],
                            nk=128 * len(kts), v=[(kt, 256 + 64 * (s % 2)) for kt in kts]))
        for s in range(8):
            h, m = s // 2, s % 2
            out.append(dict(st=st, t=t, grp=("c", t), slot=s, qc=5 + h // 2, kc=7 + h // 2, base=64 * (h % 2) + 32 * m, K=32,
                            k0=128 * kts[0], nk=128 * len(kts), v=[(kt, 384 + 64 * h) for kt in kts]))
    return out


class Counts:

    def __init__(self, known, sems):
        self.known, self.sems, self.seen, self.n = known, sems, {}, {}

    def tick(self, name, key, by=1):
        self.n[name] = self.n.get(name, 0) + by
        assert (name, key) not in self.seen, (name, key)
        self.seen[name, key] = self.n[name]
        self.last = self.sems[name], self.n[name]
        return self.sems[name], by

    def link(self, name):
        self.n[name] = self.n.get(name, 0) + 1
        self.last = self.sems[name], self.n[name]
        return self.sems[name], 1

    def has(self, name, key):
        return (name, key) in self.known

    def at(self, name, key):
        if not self.known:
            return self.sems[name], 1
        return self.sems[name], self.known[name, key]

    def note(self, name, key, value):
        self.seen[name, key] = value

    def noted(self, name, key):
        return self.known.get((name, key), 0)


SEMAPHORES = ["small", "x_in", "hi", "lo", "raw_used", "unit", "pm_act", "pm_dve", "aux", "aux_act", "aux_dve",
              "silu_c", "adasum", "mod", "sq", "sumsq", "sd", "rinv", "xr", "hmod", "hhi", "hlo", "xres",
              "zsq", "zss", "zsd", "z", "ztr", "vcopy", "gel", "avn", "mixm", "othi", "otlo",
              "negm", "p", "pt_act", "pt_dve", "ptr", "pv", "snk", "snkx", "o", "ocs", "ocss", "ocsd", "ocn",
              "cv1", "cvd", "silu", "prod", "ghi", "glo", "lg", "lx", "lxd", "lr", "la", "lm", "ls", "lh", "cstdma", "rowsdma", "mixdma", "biasdma",
              "act_chain", "dve_chain", "pool_chain", "outd", "prep", "prepa"]


def build(nc, A, known):
    with ExitStack() as stack:
        sems = {n: stack.enter_context(nc.semaphore("s_" + n)) for n in SEMAPHORES}
        raw_in = [stack.enter_context(nc.semaphore(f"s_raw{n}")) for n in range(RAW)]
        C = Counts(known, sems)
        tick, at = C.tick, C.at

        cursor = [16512]

        def sb(name, cols, dt=F32, offset=None):
            if offset is None:
                offset = cursor[0]
                cursor[0] += -(-cols * 4 // 32) * 32
            return nc.alloc_sbuf_tensor_at(name, [P, cols], dt, offset=offset)

        raw = sb("raw", RAW * UMAX)
        whi = sb("whi", SPLIT * UMAX, F32R)
        wlo = sb("wlo", SPLIT * UMAX, F32R)
        acc = sb("acc", 2 * 2 * 512)
        X = sb("X", KD * 512)
        Hhi = sb("Hhi", KD * 512, F32R)
        Hlo = sb("Hlo", KD * 512, F32R)
        T = sb("T", 4 * 512)
        reg0 = cursor[0]
        cursor[0] += 2 * HALF * 512 * 4
        Ghi = sb("Ghi", HALF * 512, F32R, reg0)
        Glo = sb("Glo", HALF * 512, F32R, reg0 + HALF * 512 * 4)
        zu = sb("zu", 2048, F32, reg0)
        QT = sb("QT", 9 * 512, F32, reg0 + 8192)
        vt = sb("vt", 4 * 640, F32, reg0 + 26624)
        ub = sb("ub", 1024, F32, reg0 + 36864)
        wsT = sb("wsT", 512, F32, reg0 + 40960)
        bsb = sb("bsb", 256, F32, reg0 + 43008)
        GT = sb("GT", NL * 256, F32, reg0)
        XR = sb("XR", NL * 256, F32, reg0 + NL * 1024)
        LA = sb("LA", NL * 256, F32, reg0 + 2 * NL * 1024)
        LU = sb("LU", NL * 256, F32, reg0 + 3 * NL * 1024)
        KT2 = sb("KT2", 2048, F32, reg0)
        VT2 = sb("VT2", 2048, F32, reg0 + 8192)
        QT2 = sb("QT2", 2048, F32, reg0 + 16384)
        bias2 = sb("bias2", 4096, F32, reg0 + 24576)
        zu2 = sb("zu2", 1024, F32, reg0 + 40960)
        rows = sb("rows", NROW)
        feat = sb("feat", NFEAT)
        cst = sb("cst", NCONST)
        mod = sb("mod", NVEC * 16)
        silc = sb("silc", 24)
        lamt = sb("lamt", 2 * 8)
        lk = sb("lk", 6 * NL)
        st8 = sb("st8", 6 * 16)
        zst = sb("zst", 2 * 3 * 32)
        eps = sb("eps", 1)
        assert cursor[0] <= 229344, cursor[0]

        PM = stack.enter_context(nc.psum_tensor("PM", [P, 2, 1024], F32))
        PX = stack.enter_context(nc.psum_tensor("PX", [P, AUXN, 512], F32))
        PO = stack.enter_context(nc.psum_tensor("PO", [P, 512], F32))

        ident = cst[:, 0:128]
        ones = cst[:, 128:256]

        def fcol(name, n):
            return feat[:, FEAT[name] + n:FEAT[name] + n + 1]

        def row(name, l):
            a, w = ROWS[name, l]
            return rows[:, a:a + w]

        def modc(v, who, k):
            n = v * 16 + who * 8 + k
            return mod[:, n:n + 1]

        def slot_raw(n, size):
            return raw[:, (n % RAW) * UMAX:(n % RAW) * UMAX + size]

        def wslot(buf, i, size, off=0):
            a = (i % SPLIT) * UMAX + off
            return buf[:, a:a + size]

        def usize(u):
            return u["kt"] * u["cols"]

        def raw_ready(eng, key):
            n = RAW_AT[key]
            eng.wait_ge(raw_in[n % RAW], 16 * (n // RAW + 1))

        def pm(i, a, n):
            return PM[:, i % 2, a:a + n]

        def aux(key, a=0, n=512):
            b = C.noted("bank", key)
            return PX[:, b, a:a + n]

        def view(ap, pattern, **k):
            return ap.rearrange(pattern, **k)

        def bcast(ap, shape):
            return ap.to_broadcast(shape)

        def tslot(n, w=512):
            return T[:, n * 512:n * 512 + w]

        def heads(u):
            l = int(u["st"][1]) if u["st"][0] == "L" else 0
            return {"bq0": (64, 4, "bq", "b"), "bq1": (64, 4, "bq", "b"), "bkv": (64, 2, "bk", "b"), "cq": (32, 8, "cq", "c"),
                    "ck": (32, 8, "ck", "c"), "k": (64, 4, "k2", None), "q": (64, 4, "q2", None)}[u["kind"]] + (l,)

        def qk_halves(u):
            return {"bq0": [0, 1], "bq1": [2, 3], "bkv": [4], "cq": [5, 6], "ck": [7, 8]}.get(u["kind"]) or \
                [2 * u["idx"], 2 * u["idx"] + 1]

        def zbuf(u):
            n = u["i"] % 2
            if u["st"][0] == "L":
                return zu[:, n * 1024:n * 1024 + 256 * u["nt"]]
            return zu2[:, n * 512:n * 512 + 512]

        def is_qk(u):
            return u["kind"] in ("bq0", "bq1", "bkv", "cq", "ck", "k", "q")

        def rinv_of(n, W):
            return tslot(2) if W == 512 else X[:, 7 * 512 + 256:8 * 512]

        def moving(u):
            if u["kind"] in ("down", "w2"):
                return Ghi, Glo, u["T"]
            if u["st"] == "L1" and u["idx"] < 8 and u["kind"] not in ("out", "up", "down"):
                return Hhi, Hlo, 512
            return Hhi, Hlo, u["T"]

        def ptiles(st):
            base, w = (zu, 512) if st != "M1" else (zu2, 256)
            return ([base[:, n * w:(n + 1) * w] for n in range(2)], [base[:, (2 + n) * w:(3 + n) * w] for n in range(2)])

        def stat(what, g, a=0, n=8):
            o = what * 16 + (g % 2) * 8
            return st8[:, o + a:o + a + n]

        NEGM, DEN, SNK, REC = range(4)
        NTOK = {"L0": 4, "L1": 2, "M1": 2}
        groups = {}
        for s in ("L0", "L1", "M1"):
            for t in attention_tiles(s):
                groups.setdefault((s, t["grp"]), len(groups))

        block = stack.enter_context(nc.Block())

        @block.sync
        def _(sp):
            sp.dma_start(feat[:, :], A["feat"]).then_inc(*tick("small", "feat", 16))
            sp.dma_start(X[:, :], A["x0"]).then_inc(*tick("x_in", 0, 16))
            for n, (what, k) in enumerate(RAW_ORDER):
                if n >= RAW:
                    sp.wait_ge(*at("raw_used", n - RAW))
                if what == "ada":
                    src, size = A["ada"][k], UMAX
                else:
                    u = UNITS[k]
                    size = usize(u)
                    src = A[{"L": "wl", "M": "wm", "K": "wm"}[u["st"][0]] + f"_{size}"][A["place"][k]]
                sp.dma_start(slot_raw(n, size), src).then_inc(raw_in[n % RAW], 16)
            for c in range(KD):
                sp.wait_ge(*at("xres", ("M1", "last", c)))
                sp.dma_start(A["out"][:, c, :], X[:, c * 512:c * 512 + 256]).then_inc(*tick("outd", c, 16))
            sp.wait_ge(*at("outd", KD - 1))

        def pool_prod(pool, u):
            i, W = u["i"], u["T"]
            g, val = tslot(2 * (i % 2), W), tslot(2 * (i % 2) + 1, W)
            pool.wait_ge(*at("silu", i))
            pool.wait_ge(*at("cvd", (i, 1)))
            pool.tensor_tensor(g, g, val, ALU.mult).then_inc(*tick("prod", i))

        @block.gpsimd
        def _(pool):
            pool.dma_start(cst[:, :], A["cst"]).then_inc(*tick("cstdma", 0, 16))
            pool.dma_start(rows[:, :], bass.AP.partition_broadcast(A["rows"], P)).then_inc(*tick("rowsdma", 0, 16))

            def load_mix(l):
                pool.dma_start(wsT[:, :], A["wsT"][l]).then_inc(*tick("mixdma", ("wsT", l), 16))
                for hh in range(2):
                    src = A["abs"][l, hh]
                    pool.dma_start(bsb[64 * hh:64 * hh + 64, :], bass.AP.partition_broadcast(src, 64))\
                        .then_inc(*tick("mixdma", ("bs", l, hh), 16))

            load_mix(0)
            for step in PROGRAM:
                if step[0] == "norm":
                    _, n, st, W = step
                    v = vec_base(st) + (3 if n in (1, 3, 5, 8) else 0)
                    if step[1] == 2:
                        pool.wait_ge(*at("unit", first_of("bq0", "L1") - 1))
                        load_mix(1)
                    if n == 6:
                        pool.wait_ge(*at("unit", first_of("k", "KV") - 1))
                        src = A["bias"]
                        pool.dma_start(view(bias2[:, :], "p (h k) -> p h k", h=16), src).then_inc(*tick("biasdma", 0, 16))
                    pool.wait_ge(*at("mod", v + 1))
                    for k in range(KD):
                        pool.wait_ge(*at("xr", (n, k)))
                        for who in range(W // 256):
                            t = tslot(k % 2)[:, who * 256:who * 256 + 256]
                            ins = pool.tensor_scalar(t, t, modc(v + 1, who, k), modc(v, who, k), ALU.mult, ALU.add)
                        ins.then_inc(*tick("hmod", (n, k)))
                if step[0] == "unit":
                    u = UNITS[step[1]]
                    i = u["i"]
                    if u["kind"] == "up" and u["idx"] % HALF > 0:
                        pool_prod(pool, UNITS[i - 1])
                    if u["kind"] == "down" and u["idx"] % KD == 0:
                        pool_prod(pool, UNITS[i - 1])

        @block.scalar
        def _(act):
            def link(ins):
                ins.then_inc(*C.link("act_chain"))
                act.wait_ge(*C.last)

            def split_hi(i):
                if i >= NU:
                    return
                u = UNITS[i]
                raw_ready(act, ("w", i))
                if i >= SPLIT:
                    act.wait_ge(*at("unit", i - SPLIT))
                act.activation(wslot(whi, i, usize(u)), slot_raw(RAW_AT["w", i], usize(u)), ACT.Copy)\
                    .then_inc(*tick("hi", i))

            def squares(n, chunks, W):
                for k in chunks:
                    if n:
                        act.wait_ge(*at("xres", (n, k)))
                    else:
                        act.wait_ge(*at("x_in", 0))
                    if k >= 2:
                        act.wait_ge(*at("sumsq", (n, k - 2)))
                    act.activation(tslot(2 + k % 2, W), X[:, k * 512:k * 512 + W], ACT.Square).then_inc(*tick("sq", (n, k)))

            act.wait_ge(*at("small", "feat"))
            act.activation(silc[:, :], feat[:, FEAT["c"]:FEAT["c"] + 24], ACT.Silu).then_inc(*tick("silu_c", 0))
            act.wait_ge(*at("prep", "lam"))
            act.activation(view(lamt[:, :], "p (l c) -> p l c", l=2)[:, :, 2:4], view(lamt[:, :], "p (l c) -> p l c", l=2)[:, :, 0:2],
                           ACT.Exp).then_inc(*tick("prepa", "lam"))
            act.wait_ge(*at("prep", "lru"))
            act.activation(lk[:, 2 * NL:3 * NL], lk[:, NL:2 * NL], ACT.Exp, scale=-1.0).then_inc(*tick("prepa", "lru"))
            squares(0, range(KD), 512)

            def ffn_stage2(u):
                i, W = u["i"], u["T"]
                g = tslot(2 * (i % 2), W)
                act.wait_ge(*at("cvd", (i, 0)))
                act.activation(g, g, ACT.Silu).then_inc(*tick("silu", i))

            def ffn_stage3(u):
                i, W = u["i"], u["T"]
                k = u["idx"] % HALF
                act.wait_ge(*at("prod", i))
                act.activation(Ghi[:, k * W:(k + 1) * W], tslot(2 * (i % 2), W), ACT.Copy).then_inc(*tick("ghi", i))

            def evac(u):
                i, W, kind = u["i"], u["T"], u["kind"]
                act.wait_ge(*C.last)
                if is_qk(u):
                    d, g, _, _, _ = heads(u)
                    nt, w = u["nt"], (128 if kind == "bkv" else 256)
                    act.wait_ge(*at("unit", i))
                    src = view(pm(i, 0, nt * 256), "p (t c) -> p t c", t=nt)
                    dst = view(T[:, 0:nt * w], "p (t c) -> p t c", t=nt)
                    act.activation(dst, src[:, :, 0:w], ACT.Square).then_inc(*tick("zsq", i))
                    if kind == "bkv":
                        act.activation(view(vt[:, :], "p (t c) -> p t c", t=4)[:, 0:nt, 256:384], src[:, :, 128:256], ACT.Copy)\
                            .then_inc(*tick("vcopy", i))
                    act.wait_ge(*at("zss", i))
                    n = nt * g
                    act.activation(zst[:, 32:32 + n], zst[:, 0:n], ACT.Sqrt, scale=1.0 / d, bias=eps[:, :]).then_inc(*tick("zsd", i))
                elif kind == "cv":
                    nt = u["nt"]
                    act.wait_ge(*at("unit", i))
                    act.activation(view(vt[:, :], "p (t c) -> p t c", t=4)[:, 0:nt, 384:640],
                                   view(pm(i, 0, nt * 256), "p (t c) -> p t c", t=nt), ACT.Copy).then_inc(*tick("pm_act", i))
                elif kind == "v":
                    n = u["idx"] - 4
                    act.wait_ge(*at("unit", i))
                    act.activation(view(VT2[:, :], "p (t c) -> p t c", t=2)[:, :, n * 256:n * 256 + 256],
                                   view(pm(i, 0, 512), "p (t c) -> p t c", t=2), ACT.Copy).then_inc(*tick("pm_act", i))
                elif kind == "av":
                    nt = u["nt"]
                    act.wait_ge(*at("unit", i))
                    v = view(vt[:, :], "p (t c) -> p t c", t=4)[:, 0:nt, 0:256]
                    act.activation(v, view(pm(i, 0, nt * 256), "p (t c) -> p t c", t=nt), ACT.Gelu_apprx_tanh)\
                        .then_inc(*tick("pm_act", i))
                    act.wait_ge(*at("pm_act", i))
                    act.activation(view(T[:, 0:nt * 256], "p (t c) -> p t c", t=nt), v, ACT.Square).then_inc(*tick("zsq", i))
                    act.wait_ge(*at("zss", i))
                    act.activation(zst[:, 32:32 + 4 * nt], zst[:, 0:4 * nt], ACT.Sqrt, scale=1.0 / 64, bias=eps[:, :])\
                        .then_inc(*tick("zsd", i))
                elif kind == "au":
                    act.wait_ge(*at("unit", i))
                    act.activation(view(ub[:, 0:2 * W], "p (c t) -> p c t", c=2), view(pm(i, 0, 1024), "p (c t) -> p c t", c=2)[:, :, 0:W],
                                   ACT.Gelu_apprx_tanh).then_inc(*tick("pm_act", i))
                elif kind == "up":
                    l, j = int(u["st"][1]), u["idx"]
                    act.wait_ge(*at("unit", i))
                    for part in range(2):
                        n = j + part * NFF
                        dst = tslot(2 * (i % 2) + part, W)
                        if u["idx"] % HALF > 1:
                            act.wait_ge(*at("glo", i - 2))
                        act.activation(dst, pm(i, part * 512, W), ACT.Identity, scale=fcol("cw", (l * 3 + 1) * 44 + n),
                                       bias=fcol("cb", l * 44 + n)).then_inc(*tick("cv1", (i, part)))
                elif kind == "lin":
                    j = u["idx"]
                    act.wait_ge(*at("unit", i))
                    act.activation(GT[:, j * 256:j * 256 + 256], pm(i, 0, 256), ACT.Gelu_apprx_tanh).then_inc(*tick("pm_act", i))
                    act.activation(XR[:, j * 256:j * 256 + 256], pm(i, 512, 256), ACT.Identity, scale=fcol("lcw", 3 * NL + j),
                                   bias=fcol("lcb", j)).then_inc(*tick("lx", j))
                elif kind == "lgate":
                    act.wait_ge(*at("unit", i))
                    for c, j in enumerate(GATE_UNITS[u["idx"]]):
                        if j >= 2:
                            act.wait_ge(*at("la", j - 2))
                        r, ig, th = (T[:, (j % 2) * 1024 + a * 256:(j % 2) * 1024 + a * 256 + 256] for a in range(3))
                        link(act.activation(r, pm(i, c * 512, 256), ACT.Sigmoid, bias=fcol("lba", j)))
                        ins = act.activation(ig, pm(i, c * 512 + 256, 256), ACT.Sigmoid, bias=fcol("lbx", j))
                        if c == len(GATE_UNITS[u["idx"]]) - 1:
                            ins.then_inc(*tick("pm_act", i))
                            act.wait_ge(*at("pm_act", i))
                        else:
                            link(ins)
                        act.activation(th, r, ACT.Tanh, scale=lk[:, 5 * NL + j:5 * NL + j + 1]).then_inc(*tick("lr", j))
                elif kind == "w1":
                    act.wait_ge(*at("unit", i))
                    r, g = tslot(2 * (i % 2)), tslot(2 * (i % 2) + 1)
                    if u["idx"] % 8 >= 2:
                        act.wait_ge(*at("glo", i - 2))
                    act.activation(view(r, "p (c t) -> p c t", c=2), view(pm(i, 0, 1024), "p (c t) -> p c t", c=2)[:, :, 0:256],
                                   ACT.Relu).then_inc(*tick("pm_act", i))
                    act.wait_ge(*at("pm_act", i))
                    act.activation(g, r, ACT.Square).then_inc(*tick("silu", i))
                    act.wait_ge(*at("silu", i))
                    k = u["idx"] % 8
                    act.activation(Ghi[:, k * 512:k * 512 + 512], g, ACT.Copy).then_inc(*tick("ghi", i))
                n = fed_norm(u)
                if n is not None:
                    squares(n, chunks_of(u), 512 if u["st"] == "L0" or n == 2 else 256)

            def attn(st):
                tiles = attention_tiles(st)
                Ps, PTs = ptiles(st)
                nt = NTOK[st]
                if st != "M1":
                    for j in range(2):
                        for tp in range(nt // 2):
                            act.wait_ge(*at("mixm", (st, j, tp)))
                            W = 128 * nt
                            act.activation(Hhi[:, j * W + tp * 256:j * W + tp * 256 + 256], tslot((j * 2 + tp) % 2, 256), ACT.Copy)\
                                .then_inc(*tick("othi", (st, "a", j, tp)))
                for n in range(len(tiles) + 4):
                    act.wait_ge(*C.last)
                    if n < len(tiles):
                        x = tiles[n]
                        g = groups[st, x["grp"]]
                        act.wait_ge(*at("negm", (st, n)))
                        if n >= 2:
                            act.wait_ge(*at("aux", ("T", st, n - 2)))
                        dst = Ps[n % 2][:, 0:x["nk"]]
                        src = dst if st == "M1" else aux(("S", st, n), 0, x["nk"])
                        ins = act.activation(dst, src, ACT.Exp, bias=stat(NEGM, g, x["slot"], 1),
                                             accum_out=stat(DEN, g, x["slot"], 1))
                        ins.then_inc(*tick("p", (st, n)))
                        if x["slot"] == 7 and x["grp"][0] == "b":
                            act.wait_ge(*at("snk", (st, n)))
                            act.activation(stat(SNK, g), stat(SNK, g), ACT.Exp).then_inc(*tick("snkx", (st, n)))
                    if 1 <= n <= len(tiles) and (n - 1) % 2 == 0:
                        x = tiles[n - 1]
                        act.wait_ge(*at("aux", ("T", st, n - 1)))
                        if n - 1 >= 2:
                            act.wait_ge(*at("pv", (st, n - 3)))
                        act.activation(PTs[(n - 1) % 2][:, 0:x["nk"]], aux(("T", st, n - 1), 0, x["nk"]), ACT.Copy)\
                            .then_inc(*tick("aux_act", ("T", st, n - 1)))
                    if n >= 4 and tiles[n - 4]["slot"] == 7 and tiles[n - 4]["grp"][0] != "c":
                        x = tiles[n - 4]
                        key = ("OT", st, x["grp"])
                        act.wait_ge(*at("aux", key))
                        c0 = 2 if st != "M1" else 4 * x["grp"][2]
                        W = 128 * nt
                        dst = view(Hhi[:, c0 * W:(c0 + 4) * W], "p (c t) -> p c t", c=4)[:, :, x["t"] * 128:x["t"] * 128 + 128]
                        act.activation(dst, view(aux(key), "p (c t) -> p c t", c=4), ACT.Copy).then_inc(*tick("othi", key))
                if st != "M1":
                    act.wait_ge(*at("o", (st, ("c", nt - 1))))
                    act.wait_ge(*at("pv", (st, len(tiles) - 1)))
                    act.activation(zu[:, 0:256 * nt], T[:, 1024:1024 + 256 * nt], ACT.Square).then_inc(*tick("ocs", st))
                    act.wait_ge(*at("ocss", st))
                    act.activation(zst[:, 32:32 + 4 * nt], zst[:, 0:4 * nt], ACT.Sqrt, scale=1.0 / 64, bias=eps[:, :])\
                        .then_inc(*tick("ocsd", st))
                    W = 128 * nt
                    for tp in range(nt // 2):
                        key = ("OC", st, tp)
                        act.wait_ge(*at("aux", key))
                        dst = view(Hhi[:, 6 * W:8 * W], "p (c t) -> p c t", c=2)[:, :, tp * 256:tp * 256 + 256]
                        act.activation(dst, view(aux(key), "p (c t) -> p c t", c=2), ACT.Copy).then_inc(*tick("othi", key))

            def root(n, W):
                act.wait_ge(*at("sumsq", (n, 7)))
                act.activation(rinv_of(n, W), PO[:, 0:W], ACT.Sqrt, scale=1.0 / D, bias=eps[:, :]).then_inc(*tick("sd", n))

            act.wait_ge(*at("prep", "eps"))
            root(0, 512)
            for i in range(2):
                split_hi(i)
            for step in PROGRAM:
                if step[0] == "norm":
                    _, n, st, W = step
                    if n not in (0, 7):
                        root(n, W)
                    for k in range(KD):
                        act.wait_ge(*at("hmod", (n, k)))
                        act.activation(Hhi[:, k * W:(k + 1) * W], tslot(k % 2, W), ACT.Copy).then_inc(*tick("hhi", (n, k)))
                elif step[0] == "attn":
                    prev = UNITS[first_of("out", step[1]) - 1]
                    attn(step[1])
                elif step[0] == "lsplit":
                    act.wait_ge(*at("unit", first_of("lgate", "M0") - 1))
                    for j in range(NL):
                        act.wait_ge(*at("lxd", j))
                        act.activation(Hhi[:, j * 256:j * 256 + 256], XR[:, j * 256:j * 256 + 256], ACT.Copy).then_inc(*tick("hhi", ("x", j)))
                elif step[0] == "lscan":
                    act.wait_ge(*at("lm", 0))
                    act.activation(XR[:, :], XR[:, :], ACT.Sqrt, scale=-1.0).then_inc(*tick("ls", 0))
                    for j in range(NL):
                        act.wait_ge(*at("lh", j))
                        act.activation(Hhi[:, j * 256:j * 256 + 256], LU[:, j * 256:j * 256 + 256], ACT.Copy).then_inc(*tick("hhi", ("y", j)))
                else:
                    u = UNITS[step[1]]
                    i = u["i"]
                    up_before = u["kind"] in ("up", "down") and UNITS[i - 1]["kind"] == "up"
                    if up_before:
                        ffn_stage2(UNITS[i - 1])
                    split_hi(i + 2)
                    if up_before:
                        ffn_stage3(UNITS[i - 1])
                    evac(u)

        @block.vector
        def _(dve):
            def link(ins):
                ins.then_inc(*C.link("dve_chain"))
                dve.wait_ge(*C.last)

            def split_lo(i):
                if i >= NU:
                    return
                u = UNITS[i]
                dve.wait_ge(*at("hi", i))
                n = RAW_AT["w", i]
                dve.tensor_tensor(wslot(wlo, i, usize(u)), slot_raw(n, usize(u)), wslot(whi, i, usize(u)).bitcast(F32), ALU.subtract)\
                    .then_inc(*tick("raw_used", n))

            def ada(a):
                hv, part = a // 2, a % 2
                v = hv // 2
                who_c = 0 if v < 12 else 2
                n = RAW_AT["ada", a]
                raw_ready(dve, ("ada", a))
                if part == 0 and hv >= 2:
                    dve.wait_ge(*at("aux", ("ada", hv - 2)))
                for k in range(4):
                    w = slot_raw(n, UMAX)[:, k * 512:k * 512 + 512]
                    kk = part * 4 + k
                    for who in range(2 if v < CTXV else 1):
                        s = silc[:, (who_c + who) * 8 + kk:(who_c + who) * 8 + kk + 1]
                        dst = acc[:, (hv % 2) * 1024 + who * 512:(hv % 2) * 1024 + who * 512 + 512]
                        if kk == 0:
                            ins = dve.tensor_scalar(dst, w, s, None, ALU.mult)
                        else:
                            ins = dve.scalar_tensor_tensor(out=dst, in0=w, scalar=s, in1=dst, op0=ALU.mult, op1=ALU.add)
                        last = k == 3 and who == (1 if v < CTXV else 0)
                        if last:
                            ins.then_inc(*tick("raw_used", n))
                        else:
                            ins.then_inc(*C.link("dve_chain"))
                    dve.wait_ge(*C.last)

            def ada_done(hv):
                v, half = hv // 2, hv % 2
                key = ("ada", hv)
                dve.wait_ge(*at("aux", key))
                nw = 2 if v < CTXV else 1
                base = {0: 0, 1: 6, 2: 12, 3: 18, 4: 20}[0 if v < 6 else 1 if v < 12 else 2 if v < 18 else 3 if v < 20 else 4]
                kind = MODTYPE[v - base]
                dst = view(mod[:, v * 16:v * 16 + 16], "p (w k) -> p w k", w=2)[:, 0:nw, half * 4:half * 4 + 4]
                srcv = view(aux(key, 0, 8), "p (w k) -> p w k", w=2)[:, 0:nw, :]
                bia = feat[:, FEAT["bada"] + v * 8 + half * 4:FEAT["bada"] + v * 8 + half * 4 + 4].unsqueeze(1).to_broadcast([P, nw, 4])
                ins = dve.tensor_tensor(dst, srcv, bia, ALU.add)
                if kind == "scale":
                    norm = {1: 0, 4: 1, 7: 2, 10: 3, 13: 4, 16: 5, 19: 6, 21: 7, 24: 8}[v]
                    ins.then_inc(*tick("aux_dve", key))
                    dve.wait_ge(*at("aux_dve", key))
                    g = feat[:, FEAT["norm"] + norm * 8 + half * 4:FEAT["norm"] + norm * 8 + half * 4 + 4].unsqueeze(1).to_broadcast([P, nw, 4])
                    ins = dve.scalar_tensor_tensor(out=dst, in0=dst, scalar=1.0, in1=g, op0=ALU.add, op1=ALU.mult)
                    ins.then_inc(*tick("mod", v if half else ("half", v)))
                else:
                    ins.then_inc(*tick("aux_dve", key))

            def mod_ready(v):
                return at("aux_dve", ("ada", 2 * v + 1))

            dve.memset(eps[:, :], EPS).then_inc(*tick("prep", "eps"))
            dve.wait_ge(*at("rowsdma", 0))
            dve.wait_ge(*at("cstdma", 0))
            for l in range(2):
                lam = view(row("lam", l), "p (a b d) -> p a b d", a=2, b=2)
                link(dve.tensor_tensor(view(T[:, l * 64:l * 64 + 64], "p (a d) -> p a d", a=2), lam[:, :, 0, :], lam[:, :, 1, :], ALU.mult))
                ins = dve.reduce_sum(lamt[:, l * 8:l * 8 + 2], view(T[:, l * 64:l * 64 + 64], "p (a d) -> p a d", a=2), AX)
                if l == 0:
                    link(ins)
                else:
                    ins.then_inc(*tick("prep", "lam"))
                link(dve.tensor_scalar(row("bq", l), row("bq", l), 64 ** -0.5, None, ALU.mult))
                link(dve.tensor_scalar(row("cq", l), row("cq", l), 32 ** -0.5, None, ALU.mult))
                init = 0.8 - 0.6 * math.exp(-0.3 * l)
                link(dve.tensor_scalar(row("sub", l), row("sub", l), 1.0 - init, None, ALU.mult))
            link(dve.tensor_scalar(row("q2", 0), row("q2", 0), 64 ** -0.5, None, ALU.mult))
            dve.wait_ge(*at("prepa", "lam"))
            for l in range(2):
                init = 0.8 - 0.6 * math.exp(-0.3 * l)
                link(dve.tensor_tensor(lamt[:, l * 8 + 4:l * 8 + 5], lamt[:, l * 8 + 2:l * 8 + 3], lamt[:, l * 8 + 3:l * 8 + 4], ALU.subtract))
                link(dve.tensor_scalar(lamt[:, l * 8 + 5:l * 8 + 6], lamt[:, l * 8 + 4:l * 8 + 5], init, None, ALU.add))
            dve.wait_ge(*at("small", "feat"))
            lamf = feat[:, FEAT["lam"]:FEAT["lam"] + NL]
            neg, ab, e, w, w2, res = (lk[:, a * NL:(a + 1) * NL] for a in range(6))
            link(dve.tensor_scalar(neg, lamf, -1.0, None, ALU.mult))
            dve.tensor_tensor(ab, neg, lamf, ALU.max).then_inc(*tick("prep", "lru"))
            dve.wait_ge(*at("prepa", "lru"))
            link(dve.tensor_scalar(w2, e, 2.0, None, ALU.add))
            link(dve.reciprocal(res, w2))
            link(dve.tensor_tensor(w, e, res, ALU.mult))
            link(dve.tensor_tensor(w2, w, w, ALU.mult))
            link(dve.tensor_scalar(res, w2, 1.0 / 19, 1.0 / 17, ALU.mult, ALU.add))
            for m in range(7, -1, -1):
                link(dve.tensor_tensor(res, res, w2, ALU.mult))
                link(dve.tensor_scalar(res, res, 1.0 / (2 * m + 1), None, ALU.add))
            link(dve.tensor_tensor(res, res, w, ALU.mult))
            link(dve.tensor_scalar(neg, neg, 0.0, 4.0, ALU.max, ALU.mult))
            link(dve.scalar_tensor_tensor(out=res, in0=res, scalar=8.0, in1=neg, op0=ALU.mult, op1=ALU.add))

            def head_norm(u):
                i = u["i"]
                d, g, gain, rot, l = heads(u)
                nt, w = u["nt"], (128 if u["kind"] == "bkv" else 256)
                n = nt * g
                dve.wait_ge(*at("zsq", i))
                dve.reduce_sum(zst[:, 0:n], view(T[:, 0:nt * w], "p (g d) -> p g d", d=d), AX).then_inc(*tick("zss", i))
                dve.wait_ge(*at("zsd", i))
                link(dve.reciprocal(zst[:, 64:64 + n], zst[:, 32:32 + n]))
                z = zbuf(u)
                if i >= 2 and is_qk(UNITS[i - 2]):
                    for h in range(len(qk_halves(UNITS[i - 2]))):
                        dve.wait_ge(*at("aux", ("qkT", i - 2, h)))
                z4 = view(z, "p (t g d) -> p t g d", t=nt, d=d)
                src4 = view(pm(i, 0, nt * 256), "p (t g d) -> p t g d", t=nt, d=d)
                r4 = view(zst[:, 64:64 + n], "p (t g) -> p t g", t=nt).unsqueeze(3).to_broadcast([P, nt, g, d])
                ins = dve.tensor_tensor(z4[:, :, 0:g, :], src4[:, :, 0:g, :], r4, ALU.mult)
                ins.then_inc(*tick("pm_dve", i))
                dve.wait_ge(*at("pm_dve", i))
                g4 = row(gain, l).unsqueeze(1).unsqueeze(1).to_broadcast([P, nt, g, d])
                ins = dve.tensor_tensor(z4[:, :, 0:g, :], z4[:, :, 0:g, :], g4, ALU.mult)
                if rot is None:
                    ins.then_inc(*tick("z", i))
                    return
                link(ins)
                f = d // 4
                ct, stb = (CONST["cb"], CONST["sb"]) if rot == "b" else (CONST["cc"], CONST["sc"])
                sw = T[:, 1024:1024 + 2 * w]
                for t in range(2):
                    zz = view(z[:, t * 256:t * 256 + w], "p (g a h f) -> p g a h f", a=2, h=2, f=f)
                    ss = view(sw[:, t * w:(t + 1) * w], "p (g a h f) -> p g a h f", a=2, h=2, f=f)
                    sn = view(cst[:, stb + t * d:stb + (t + 1) * d], "p (a h f) -> p a h f", a=2, h=2)
                    for h in range(2):
                        dve.tensor_tensor(ss[:, :, :, h, :], zz[:, :, :, 1 - h, :],
                                          sn[:, :, h, :].unsqueeze(1).to_broadcast([P, g, 2, f]), ALU.mult)\
                            .then_inc(*C.link("dve_chain"))
                dve.wait_ge(*C.last)
                for t in range(2):
                    zg = view(z[:, t * 256:t * 256 + w], "p (g d) -> p g d", d=d)
                    ins = dve.tensor_tensor(zg, zg, cst[:, ct + t * d:ct + (t + 1) * d].unsqueeze(1).to_broadcast([P, g, d]), ALU.mult)
                    ins.then_inc(*C.link("dve_chain"))
                dve.wait_ge(*C.last)
                zx = view(z[:, 0:512], "p (t c) -> p t c", t=2)[:, :, 0:w]
                dve.tensor_tensor(zx, zx, view(sw, "p (t c) -> p t c", t=2), ALU.add).then_inc(*tick("z", i))

            def qk_copy(u):
                i, nt = u["i"], u["nt"]
                for h, c in enumerate(qk_halves(u)):
                    key = ("qkT", i, h)
                    dve.wait_ge(*at("aux", key))
                    if u["st"][0] == "L":
                        dst = QT[:, c * 512:c * 512 + nt * 128]
                    else:
                        dst = (KT2 if u["kind"] == "k" else QT2)[:, c * 256:c * 256 + 256]
                    dve.tensor_copy(dst, aux(key, 0, nt * 128)).then_inc(*tick("aux_dve", key))

            def residual(u):
                i, W = u["i"], u["T"]
                st = u["st"]
                v = vec_base(st) + (2 if u["kind"] in ("out", "lout") else 5)
                n = fed_norm(u)
                final = u["kind"] == "w2" and st == "M1" and u["idx"] >= KD
                dve.wait_ge(*at("unit", i))
                dve.wait_ge(*mod_ready(v))
                cs = chunks_of(u)
                for m, c in enumerate(cs):
                    for who in range(W // 256):
                        dst = X[:, c * 512 + who * 256:c * 512 + who * 256 + 256]
                        ins = dve.scalar_tensor_tensor(out=dst, in0=pm(i, m * 512 + who * 256, 256), scalar=modc(v, who, c),
                                                       in1=dst, op0=ALU.mult, op1=ALU.add)
                        lastw = who == W // 256 - 1
                        if lastw and n is not None:
                            ins.then_inc(*tick("xres", (n, c)))
                        elif lastw and final:
                            ins.then_inc(*tick("xres", (st, "last", c)))
                        elif lastw and m == len(cs) - 1:
                            ins.then_inc(*tick("pm_dve", i))
                            dve.wait_ge(*at("pm_dve", i))

            def evac(u):
                i, W, kind = u["i"], u["T"], u["kind"]
                dve.wait_ge(*C.last)
                if is_qk(u):
                    head_norm(u)
                elif kind == "av":
                    nt = u["nt"]
                    dve.wait_ge(*at("zsq", i))
                    dve.reduce_sum(zst[:, 0:4 * nt], view(T[:, 0:nt * 256], "p (g d) -> p g d", d=64), AX).then_inc(*tick("zss", i))
                    dve.wait_ge(*at("zsd", i))
                    link(dve.reciprocal(zst[:, 64:64 + 4 * nt], zst[:, 32:32 + 4 * nt]))
                    v4 = view(view(vt[:, :], "p (t c) -> p t c", t=4)[:, 0:nt, 0:256], "p t (g d) -> p t g d", d=64)
                    r4 = view(zst[:, 64:64 + 4 * nt], "p (t g) -> p t g", t=nt).unsqueeze(3).to_broadcast([P, nt, 4, 64])
                    dve.tensor_tensor(v4, v4, r4, ALU.mult).then_inc(*tick("avn", i))
                elif kind in ("out", "down", "lout", "w2"):
                    residual(u)
                    return
                elif kind == "up":
                    l, j = int(u["st"][1]), u["idx"]
                    ns = W // 256
                    for part in range(2):
                        n = j + part * NFF
                        dve.wait_ge(*at("cv1", (i, part)))
                        ps = view(pm(i, part * 512, W), "p (s t) -> p s t", s=ns)
                        y = view(tslot(2 * (i % 2) + part, W), "p (s t) -> p s t", s=ns)
                        link(dve.scalar_tensor_tensor(out=y[:, :, 1:256], in0=ps[:, :, 0:255], scalar=fcol("cw", (l * 3 + 0) * 44 + n),
                                                      in1=y[:, :, 1:256], op0=ALU.mult, op1=ALU.add))
                        dve.scalar_tensor_tensor(out=y[:, :, 0:255], in0=ps[:, :, 1:256], scalar=fcol("cw", (l * 3 + 2) * 44 + n),
                                                 in1=y[:, :, 0:255], op0=ALU.mult, op1=ALU.add).then_inc(*tick("cvd", (i, part)))
                elif kind == "lin":
                    j = u["idx"]
                    dve.wait_ge(*at("lx", j))
                    for s in range(1, 4):
                        y = XR[:, j * 256 + s:j * 256 + 256]
                        ins = dve.scalar_tensor_tensor(out=y, in0=pm(i, 512, 256 - s), scalar=fcol("lcw", (3 - s) * NL + j), in1=y,
                                                       op0=ALU.mult, op1=ALU.add)
                        if s < 3:
                            link(ins)
                        else:
                            ins.then_inc(*tick("lxd", j))
                elif kind == "lgate":
                    for j in GATE_UNITS[u["idx"]]:
                        dve.wait_ge(*at("lr", j))
                        base = (j % 2) * 1024
                        ig, th, s = (T[:, base + a * 256:base + a * 256 + 256] for a in (1, 2, 3))
                        a_, u_, x_ = (b[:, j * 256:j * 256 + 256] for b in (LA, LU, XR))
                        link(dve.tensor_scalar(a_, th, 1.0, None, ALU.add))
                        link(dve.reciprocal(s, a_))
                        link(dve.scalar_tensor_tensor(out=s, in0=s, scalar=2.0, in1=th, op0=ALU.mult, op1=ALU.mult))
                        link(dve.tensor_scalar(a_, s, -1.0, 1.0, ALU.mult, ALU.add))
                        link(dve.tensor_tensor(u_, ig, x_, ALU.mult))
                        dve.scalar_tensor_tensor(out=x_, in0=s, scalar=2.0, in1=s, op0=ALU.subtract, op1=ALU.mult).then_inc(*tick("la", j))
                elif kind == "w1":
                    dve.wait_ge(*at("ghi", i))
                    k = u["idx"] % 8
                    dve.tensor_tensor(Glo[:, k * 512:k * 512 + 512], tslot(2 * (i % 2) + 1), Ghi[:, k * 512:k * 512 + 512].bitcast(F32),
                                      ALU.subtract).then_inc(*tick("glo", i))

            def ffn_lo(u):
                i, W = u["i"], u["T"]
                k = u["idx"] % HALF
                dve.wait_ge(*at("ghi", i))
                dve.tensor_tensor(Glo[:, k * W:(k + 1) * W], tslot(2 * (i % 2), W), Ghi[:, k * W:(k + 1) * W].bitcast(F32), ALU.subtract)\
                    .then_inc(*tick("glo", i))

            def attn(st):
                tiles = attention_tiles(st)
                Ps, PTs = ptiles(st)
                nt = NTOK[st]
                W = 128 * nt
                if st != "M1":
                    l = int(st[1])
                    dve.wait_ge(*at("mixdma", ("bs", l, 1)))
                    dve.wait_ge(*at("pm_act", first_of("au", st)))
                    for j in range(2):
                        for tp in range(nt // 2):
                            key = ("mix", st, j, tp)
                            dve.wait_ge(*C.last)
                            dve.wait_ge(*at("aux", key))
                            m = tslot((j * 2 + tp) % 2, 256)
                            for hh in range(2):
                                q = slice(64 * hh, 64 * hh + 64)
                                src = PX[q, C.noted("bank", key), :].rearrange("p (t g c) -> p t g c", t=2, g=2)[:, :, hh, :]
                                bs = bsb[q, j * 128:j * 128 + 128].unsqueeze(1).to_broadcast([64, 2, 128])
                                mm = m[q, :].rearrange("p (t c) -> p t c", t=2)
                                ins = dve.tensor_tensor(mm, src, bs, ALU.add)
                                if hh == 0:
                                    link(ins)
                                else:
                                    ins.then_inc(*tick("aux_dve", key))
                            dve.wait_ge(*at("aux_dve", key))
                            dve.tensor_tensor(m, m, ub[:, j * W + tp * 256:j * W + tp * 256 + 256], ALU.mult).then_inc(*tick("mixm", (st, j, tp)))
                            dve.wait_ge(*at("othi", (st, "a", j, tp)))
                            o = j * W + tp * 256
                            dve.tensor_tensor(Hlo[:, o:o + 256], m, Hhi[:, o:o + 256].bitcast(F32), ALU.subtract)\
                                .then_inc(*tick("otlo", (st, "a", j, tp)))
                for n in range(len(tiles) + 4):
                    dve.wait_ge(*C.last)
                    if n < len(tiles):
                        x = tiles[n]
                        g, s = groups[st, x["grp"]], x["slot"]
                        key = ("S", st, n)
                        dve.wait_ge(*at("aux", key))
                        src = aux(key, 0, x["nk"])
                        if st == "M1":
                            if n >= 2:
                                dve.wait_ge(*at("aux", ("T", st, n - 2)))
                            p = Ps[n % 2][:, 0:x["nk"]]
                            dve.wait_ge(*at("biasdma", 0))
                            b = bias2[:, x["h"] * 256 + 256 - x["nk"]:x["h"] * 256 + 256]
                            dve.tensor_tensor(p, src, b, ALU.add).then_inc(*tick("aux_dve", key))
                            dve.wait_ge(*at("aux_dve", key))
                            link(dve.memset(p[0:64, x["nk"] - 64:x["nk"]], NEG))
                            dve.tensor_reduce(stat(NEGM, g, s, 1), p, AX, ALU.max, negate=True).then_inc(*tick("negm", (st, n)))
                        elif x["grp"][0] == "b":
                            link(dve.tensor_reduce(stat(REC, g, s, 1), src, AX, ALU.max))
                            sk = row("sink", int(st[1]))[:, s:s + 1]
                            dve.tensor_scalar(stat(NEGM, g, s, 1), stat(REC, g, s, 1), sk, -1.0, ALU.max, ALU.mult)\
                                .then_inc(*tick("negm", (st, n)))
                            if s == 7:
                                dve.wait_ge(*at("negm", (st, n)))
                                dve.tensor_tensor(stat(SNK, g), stat(NEGM, g), row("sink", int(st[1])), ALU.add).then_inc(*tick("snk", (st, n)))
                        else:
                            dve.tensor_reduce(stat(NEGM, g, s, 1), src, AX, ALU.max, negate=True).then_inc(*tick("negm", (st, n)))
                    if 1 <= n <= len(tiles) and (n - 1) % 2 == 1:
                        x = tiles[n - 1]
                        dve.wait_ge(*at("aux", ("T", st, n - 1)))
                        if n - 1 >= 2:
                            dve.wait_ge(*at("pv", (st, n - 3)))
                        dve.tensor_copy(PTs[(n - 1) % 2][:, 0:x["nk"]], aux(("T", st, n - 1), 0, x["nk"]))\
                            .then_inc(*tick("aux_dve", ("T", st, n - 1)))
                    if 2 <= n < len(tiles) + 2 and tiles[n - 2]["slot"] == 7:
                        x = tiles[n - 2]
                        grp = x["grp"]
                        g = groups[st, grp]
                        dve.wait_ge(*at("p", (st, n - 2)))
                        if grp[0] == "b":
                            dve.wait_ge(*at("snkx", (st, n - 2)))
                            link(dve.tensor_tensor(stat(DEN, g), stat(DEN, g), stat(SNK, g), ALU.add))
                        link(dve.reciprocal(stat(REC, g), stat(DEN, g)))
                        if grp[0] == "c":
                            odd = view(stat(REC, g), "p (h m) -> p h m", m=2)[:, :, 1]
                            link(dve.tensor_scalar(odd, odd, lamt[:, int(st[1]) * 8 + 5:int(st[1]) * 8 + 6], None, ALU.mult))
                        dve.wait_ge(*at("pv", (st, n - 2)))
                        ob = tslot(g % 2)
                        if g >= 2 and grp[0] != "c":
                            prev = [k for k, v in groups.items() if v == g - 2][0]
                            if prev[0] == st:
                                dve.wait_ge(*at("aux", ("OT", st, prev[1])))
                        ins = dve.tensor_tensor(view(ob, "p (s d) -> p s d", s=8), view(PO[:, :], "p (s d) -> p s d", s=8),
                                                stat(REC, g).unsqueeze(2).to_broadcast([P, 8, 64]), ALU.mult)
                        ins.then_inc(*tick("pm_dve", ("PO", st, grp)))
                        if grp[0] == "c":
                            dve.wait_ge(*at("pm_dve", ("PO", st, grp)))
                            o4 = view(ob, "p (h m d) -> p h m d", h=4, m=2)
                            oc = view(T[:, 1024 + x["t"] * 256:1024 + x["t"] * 256 + 256], "p (h d) -> p h d", h=4)
                            dve.tensor_tensor(oc, o4[:, :, 0, :], o4[:, :, 1, :], ALU.subtract).then_inc(*tick("o", (st, grp)))
                    if n >= 4 and tiles[n - 4]["slot"] == 7 and tiles[n - 4]["grp"][0] != "c":
                        x = tiles[n - 4]
                        key = ("OT", st, x["grp"])
                        dve.wait_ge(*at("othi", key))
                        c0 = 2 if st != "M1" else 4 * x["grp"][2]
                        dst, hi = (view(b[:, c0 * W:(c0 + 4) * W], "p (c t) -> p c t", c=4)[:, :, x["t"] * 128:x["t"] * 128 + 128]
                                   for b in (Hlo, Hhi))
                        dve.tensor_tensor(dst, view(aux(key), "p (c t) -> p c t", c=4), hi.bitcast(F32), ALU.subtract)\
                            .then_inc(*tick("aux_dve", key))
                if st != "M1":
                    l = int(st[1])
                    dve.wait_ge(*at("ocs", st))
                    dve.reduce_sum(zst[:, 0:4 * nt], view(zu[:, 0:256 * nt], "p (g d) -> p g d", d=64), AX).then_inc(*tick("ocss", st))
                    dve.wait_ge(*at("ocsd", st))
                    link(dve.reciprocal(zst[:, 64:64 + 4 * nt], zst[:, 32:32 + 4 * nt]))
                    oc = view(T[:, 1024:1024 + 256 * nt], "p (g d) -> p g d", d=64)
                    link(dve.tensor_tensor(oc, oc, zst[:, 64:64 + 4 * nt].unsqueeze(2).to_broadcast([P, 4 * nt, 64]), ALU.mult))
                    dve.tensor_tensor(oc, oc, row("sub", l).unsqueeze(1).to_broadcast([P, 4 * nt, 64]), ALU.mult).then_inc(*tick("ocn", st))
                    for tp in range(nt // 2):
                        key = ("OC", st, tp)
                        dve.wait_ge(*at("othi", key))
                        dst, hi = (view(b[:, 6 * W:8 * W], "p (c t) -> p c t", c=2)[:, :, tp * 256:tp * 256 + 256] for b in (Hlo, Hhi))
                        dve.tensor_tensor(dst, view(aux(key), "p (c t) -> p c t", c=2), hi.bitcast(F32), ALU.subtract)\
                            .then_inc(*tick("aux_dve", key))

            dve.wait_ge(*at("sd", 0))
            dve.reciprocal(rinv_of(0, 512), rinv_of(0, 512)).then_inc(*tick("rinv", 0))
            dve.wait_ge(*at("silu_c", 0))
            for hv in range(4):
                ada(2 * hv)
                ada(2 * hv + 1)
                if hv >= 1:
                    ada_done(hv - 1)
            split_lo(0)
            split_lo(1)
            ada_done(3)
            for step in PROGRAM:
                if step[0] == "norm":
                    _, n, st, W = step
                    r = rinv_of(n, W)
                    if n not in (0, 7):
                        dve.wait_ge(*at("sd", n))
                        dve.reciprocal(r, r).then_inc(*tick("rinv", n))
                    dve.wait_ge(*at("rinv", n if n != 7 else 6))
                    for k in range(KD + 1):
                        if k < KD:
                            if k >= 2:
                                dve.wait_ge(*at("hhi", (n, k - 2)))
                            dve.tensor_tensor(tslot(k % 2, W), X[:, k * 512:k * 512 + W], r, ALU.mult).then_inc(*tick("xr", (n, k)))
                        if k >= 1:
                            dve.wait_ge(*at("hhi", (n, k - 1)))
                            o = (k - 1) * W
                            dve.tensor_tensor(Hlo[:, o:o + W], tslot((k - 1) % 2, W), Hhi[:, o:o + W].bitcast(F32), ALU.subtract)\
                                .then_inc(*tick("hlo", (n, k - 1)))
                            dve.wait_ge(*at("hlo", (n, k - 1)))
                elif step[0] == "attn":
                    last = UNITS[first_of("out", step[1]) - 1]
                    if is_qk(last):
                        qk_copy(last)
                    attn(step[1])
                elif step[0] == "lsplit":
                    for j in range(NL):
                        dve.wait_ge(*at("hhi", ("x", j)))
                        dve.tensor_tensor(Hlo[:, j * 256:j * 256 + 256], XR[:, j * 256:j * 256 + 256], Hhi[:, j * 256:j * 256 + 256].bitcast(F32),
                                          ALU.subtract).then_inc(*tick("hlo", ("x", j)))
                elif step[0] == "lscan":
                    dve.wait_ge(*at("la", NL - 1))
                    dve.tensor_scalar(XR[:, :], XR[:, :], -1e-30, None, ALU.min).then_inc(*tick("lm", 0))
                    dve.wait_ge(*at("ls", 0))
                    link(dve.tensor_tensor(LU[:, :], LU[:, :], XR[:, :], ALU.mult))
                    for j in range(NL):
                        a_, u_, h_, g_ = (b[:, j * 256:j * 256 + 256] for b in (LA, LU, XR, GT))
                        link(dve.tensor_tensor_scan(h_, a_, u_, 0.0, ALU.mult, ALU.add))
                        dve.tensor_tensor(u_, h_, g_, ALU.mult).then_inc(*tick("lh", j))
                        if j:
                            dve.wait_ge(*at("hhi", ("y", j - 1)))
                            o = (j - 1) * 256
                            dve.tensor_tensor(Hlo[:, o:o + 256], LU[:, o:o + 256], Hhi[:, o:o + 256].bitcast(F32), ALU.subtract)\
                                .then_inc(*tick("hlo", ("y", j - 1)))
                    dve.wait_ge(*at("hhi", ("y", NL - 1)))
                    o = (NL - 1) * 256
                    dve.tensor_tensor(Hlo[:, o:o + 256], LU[:, o:o + 256], Hhi[:, o:o + 256].bitcast(F32), ALU.subtract)\
                        .then_inc(*tick("hlo", ("y", NL - 1)))
                else:
                    u = UNITS[step[1]]
                    i = u["i"]
                    split_lo(i + 2)
                    if u["kind"] in ("up", "down") and UNITS[i - 1]["kind"] == "up":
                        ffn_lo(UNITS[i - 1])
                    evac(u)
                    if i and is_qk(UNITS[i - 1]) and u["kind"] != "out":
                        qk_copy(UNITS[i - 1])
                    for a in ADA_AT[i]:
                        ada(a)
                    for hv in REDUCE_AT[i]:
                        ada_done(hv)

        @block.tensor
        def _(pe):
            items = []
            sums = []

            def take(key):
                n = len(items)
                if n >= AUXN:
                    old = items[n - AUXN]
                    for name in ("aux_act", "aux_dve"):
                        if C.has(name, old):
                            pe.wait_ge(*at(name, old))
                    if old[0] == "S" and old[1] != "M1":
                        pe.wait_ge(*at("p", (old[1], old[2])))
                items.append(key)
                C.note("bank", key, n % AUXN)
                return PX[:, n % AUXN, :]

            def pm_free(i):
                if i >= 2:
                    u = UNITS[i - 2]
                    for name in ("pm_act", "pm_dve"):
                        if C.has(name, i - 2):
                            pe.wait_ge(*at(name, i - 2))
                    if u["kind"] == "up":
                        pe.wait_ge(*at("cvd", (i - 2, 1)))
                    if u["kind"] == "lin":
                        pe.wait_ge(*at("lxd", u["idx"]))
                    if u["kind"] == "bkv":
                        pe.wait_ge(*at("vcopy", i - 2))
                    if u["kind"] in ("out", "down", "lout", "w2"):
                        n = fed_norm(u)
                        c = chunks_of(u)[-1]
                        if n is not None:
                            pe.wait_ge(*at("xres", (n, c)))
                        elif u["st"] == "M1" and u["kind"] == "w2" and u["idx"] >= KD:
                            pe.wait_ge(*at("xres", ("M1", "last", c)))

            def three(out, st_hi, st_lo, mv_hi, mv_lo, first, last):
                pe.matmul(out, st_hi, mv_hi, start=first, stop=False)
                pe.matmul(out, st_hi, mv_lo, start=False, stop=False)
                return pe.matmul(out, st_lo, mv_hi, start=False, stop=last)

            def operand_ready(u, k):
                kind, st, idx = u["kind"], u["st"], u["idx"]
                if kind in ("bq0", "lin", "k", "q") and idx == 0:
                    n = {"L0": 0, "L1": 2, "M0": 4, "KV": 6, "M1": 7}[st]
                    pe.wait_ge(*at("hlo", (n, k)))
                elif kind == "up" and idx == 0:
                    pe.wait_ge(*at("hlo", (1 + 2 * int(st[1]), k)))
                elif kind == "w1" and idx == 0:
                    pe.wait_ge(*at("hlo", (5 if st == "M0" else 8, k)))
                elif kind == "lout" and idx == 0:
                    pe.wait_ge(*at("hlo", ("y", k)))
                elif kind == "down" and idx % KD == 0:
                    pe.wait_ge(*at("glo", u["i"] - HALF + k))
                elif kind == "w2" and idx % KD == 0:
                    if k % 2 == 0:
                        pe.wait_ge(*at("glo", u["i"] - 8 + k // 2))
                elif kind == "out" and idx == 0 and k == 0:
                    if st == "M1":
                        for t in range(2):
                            for hg in range(2):
                                pe.wait_ge(*at("aux_dve", ("OT", st, ("m", t, hg))))
                    else:
                        for tp in range(NTOK[st] // 2):
                            pe.wait_ge(*at("otlo", (st, "a", 1, tp)))
                            pe.wait_ge(*at("aux_dve", ("OC", st, tp)))
                        for t in range(NTOK[st]):
                            pe.wait_ge(*at("aux_dve", ("OT", st, ("b", t))))

            def unit(u):
                i, kt, kind = u["i"], u["kt"], u["kind"]
                pe.wait_ge(*at("raw_used", RAW_AT["w", i]))
                pm_free(i)
                mh, ml, S = moving(u)
                if "nt" in u and kind != "au":
                    for t in range(u["nt"]):
                        for k in range(kt):
                            if t == 0:
                                operand_ready(u, k)
                            o = k * S + t * 128
                            ins = three(pm(i, t * 256, 256), mh[:, o:o + 128], ml[:, o:o + 128],
                                        wslot(whi, i, 256, k * 256), wslot(wlo, i, 256, k * 256), k == 0, k == kt - 1)
                elif kind == "lgate":
                    at_ = 0
                    for c, j in enumerate(GATE_UNITS[u["idx"]]):
                        for g in range(2):
                            for m, ci in enumerate(GATES[j]):
                                pe.wait_ge(*at("hlo", ("x", ci)))
                                ins = three(pm(i, c * 512 + g * 256, 256), wslot(whi, i, 128, at_ * 128), wslot(wlo, i, 128, at_ * 128),
                                            mh[:, ci * 256:ci * 256 + 256], ml[:, ci * 256:ci * 256 + 256], m == 0, m == len(GATES[j]) - 1)
                                at_ += 1
                else:
                    W = u["T"]
                    for c in range(u["cols"] // 128):
                        for k in range(kt):
                            if c == 0:
                                operand_ready(u, k)
                            o = k * S
                            w0 = k * u["cols"] + c * 128
                            ins = three(pm(i, c * 512, W), wslot(whi, i, 128, w0), wslot(wlo, i, 128, w0),
                                        mh[:, o:o + W], ml[:, o:o + W], k == 0, k == kt - 1)
                ins.then_inc(*tick("unit", i))

            def transposes(u):
                i, nt = u["i"], u["nt"]
                z = zbuf(u)
                pe.wait_ge(*at("z", i))
                for h in range(len(qk_halves(u))):
                    key = ("qkT", i, h)
                    dst = take(key)
                    for t in range(nt):
                        ins = pe.transpose(dst[:, t * 128:t * 128 + 128], z[:, t * 256 + h * 128:t * 256 + h * 128 + 128], ident)
                    ins.then_inc(*tick("aux", key))

            def ada_sum(hv):
                key = ("ada", hv)
                v = hv // 2
                dst = take(key)
                pe.wait_ge(*at("raw_used", RAW_AT["ada", 2 * hv + 1]))
                for who in range(2 if v < CTXV else 1):
                    for c in range(4):
                        a = (hv % 2) * 1024 + who * 512 + c * 128
                        ins = pe.matmul(dst[:, who * 4 + c:who * 4 + c + 1], acc[:, a:a + 128], ones[:, 0:1], start=True, stop=True)
                ins.then_inc(*tick("aux", key))

            def sumsq(n, k, W):
                if k == 0:
                    if n in (1, 3, 8):
                        st = {1: "L0", 3: "L1", 8: "M1"}[n]
                        g = attention_tiles(st)[-1]["grp"]
                        pe.wait_ge(*at("pm_dve", ("PO", st, g)))
                    elif n:
                        pe.wait_ge(*at("sd", n - 1 if n != 8 else 6))
                pe.wait_ge(*at("sq", (n, k)))
                pe.matmul(PO[:, 0:W], ones, tslot(2 + k % 2, W), start=(k == 0), stop=(k == 7)).then_inc(*tick("sumsq", (n, k)))

            def attn(st):
                tiles = attention_tiles(st)
                Ps, PTs = ptiles(st)
                nt = NTOK[st]
                if st != "M1":
                    l = int(st[1])
                    pe.wait_ge(*at("mixdma", ("bs", l, 1)))
                    pe.wait_ge(*at("avn", first_of("av", st)))
                    for j in range(2):
                        for tp in range(nt // 2):
                            key = ("mix", st, j, tp)
                            dst = take(key)
                            for t in range(2):
                                tt = tp * 2 + t
                                ins = pe.matmul(dst[:, t * 256:t * 256 + 256], vt[:, tt * 640 + j * 128:tt * 640 + j * 128 + 128],
                                                wsT[:, j * 256:j * 256 + 256], start=True, stop=True)
                            ins.then_inc(*tick("aux", key))
                    pe.wait_ge(*at("pm_act", first_of("cv", st)))
                    pe.wait_ge(*at("vcopy", first_of("bkv", st)))
                    pe.wait_ge(*at("aux_dve", ("qkT", first_of("ck", st), 1)))
                else:
                    pe.wait_ge(*at("aux_dve", ("qkT", first_of("q", st) + 3, 1)))
                    pe.wait_ge(*at("pm_act", first_of("v", "KV") + 3))
                for n in range(len(tiles) + 4):
                    if n < len(tiles):
                        x = tiles[n]
                        key = ("S", st, n)
                        dst = take(key)
                        b, K, nk, t = x["base"], x["K"], x["nk"], x["t"]
                        q, kk, w = (QT, QT, 512) if st != "M1" else (QT2, KT2, 256)
                        mask = x["grp"][0] == "b" and t < 2
                        ins = pe.matmul(dst[:, 0:nk], q[b:b + K, x["qc"] * w + t * 128:x["qc"] * w + t * 128 + 128],
                                        kk[b:b + K, x["kc"] * w + x["k0"]:x["kc"] * w + x["k0"] + nk], start=True, stop=not mask)
                        if mask:
                            c = 128 * (1 - t)
                            ins = pe.matmul(dst[:, c:c + 128], ident, cst[:, CONST["mask"] + t * 128:CONST["mask"] + t * 128 + 128],
                                            start=False, stop=True)
                        ins.then_inc(*tick("aux", key))
                    if 1 <= n <= len(tiles):
                        x = tiles[n - 1]
                        key = ("T", st, n - 1)
                        dst = take(key)
                        pe.wait_ge(*at("p", (st, n - 1)))
                        for c in range(x["nk"] // 128):
                            ins = pe.transpose(dst[:, c * 128:c * 128 + 128], Ps[(n - 1) % 2][:, c * 128:c * 128 + 128], ident)
                        ins.then_inc(*tick("aux", key))
                    if 2 <= n < len(tiles) + 2:
                        x = tiles[n - 2]
                        m = n - 2
                        s = x["slot"]
                        if s == 0:
                            if m == 0:
                                pe.wait_ge(*at("sd", {"L0": 0, "L1": 2, "M1": 6}[st]))
                            else:
                                pe.wait_ge(*at("pm_dve", ("PO", st, tiles[m - 1]["grp"])))
                        pe.wait_ge(*at("aux_dve" if m % 2 else "aux_act", ("T", st, m)))
                        for c, (kt, off) in enumerate(x["v"]):
                            v = vt[:, kt * 640 + off:kt * 640 + off + 64] if st != "M1" else VT2[:, kt * 1024 + off:kt * 1024 + off + 64]
                            ins = pe.matmul(PO[:, s * 64:s * 64 + 64], PTs[m % 2][:, c * 128:c * 128 + 128], v,
                                            start=(c == 0), stop=(c == len(x["v"]) - 1))
                        ins.then_inc(*tick("pv", (st, m)))
                    if n >= 4 and tiles[n - 4]["slot"] == 7 and tiles[n - 4]["grp"][0] != "c":
                        x = tiles[n - 4]
                        key = ("OT", st, x["grp"])
                        dst = take(key)
                        g = groups[st, x["grp"]]
                        pe.wait_ge(*at("pm_dve", ("PO", st, x["grp"])))
                        for c in range(4):
                            ins = pe.transpose(dst[:, c * 128:c * 128 + 128], tslot(g % 2)[:, c * 128:c * 128 + 128], ident)
                        ins.then_inc(*tick("aux", key))
                if st != "M1":
                    pe.wait_ge(*at("ocn", st))
                    for tp in range(nt // 2):
                        key = ("OC", st, tp)
                        dst = take(key)
                        for c in range(2):
                            for t in range(2):
                                o = 1024 + (tp * 2 + t) * 256 + c * 128
                                ins = pe.transpose(dst[:, c * 256 + t * 128:c * 256 + t * 128 + 128], T[:, o:o + 128], ident)
                        ins.then_inc(*tick("aux", key))

            pe.wait_ge(*at("cstdma", 0))
            for k in range(KD):
                sumsq(0, k, 512)
            for hv in range(4):
                ada_sum(hv)
            late = []
            for step in PROGRAM:
                if step[0] in ("norm", "attn"):
                    for a in late:
                        sumsq(*a)
                    late = []
                if step[0] == "attn":
                    last = UNITS[first_of("out", step[1]) - 1]
                    if is_qk(last):
                        transposes(last)
                    attn(step[1])
                if step[0] == "unit":
                    u = UNITS[step[1]]
                    i = u["i"]
                    unit(u)
                    for a in late:
                        sumsq(*a)
                    late = []
                    if i and is_qk(UNITS[i - 1]) and u["kind"] != "out":
                        transposes(UNITS[i - 1])
                    for hv in REDUCE_AT[i]:
                        ada_sum(hv)
                    n = fed_norm(u)
                    if n is not None:
                        late = [(n, k, 512 if u["st"] == "L0" or n == 2 else 256) for k in chunks_of(u)]
        return C.seen


def _units_of(w, kt, order=None):
    K, N = w.shape
    out = []
    for cols in order:
        part = w[:, cols]
        for a in range(0, K // P, kt):
            blk = part[a * P:(a + kt) * P].reshape(kt, P, len(cols))
            out.append(blk.transpose(1, 0, 2).reshape(P, kt * len(cols)))
    return out


def _lay_out(I):
    f = {k: np.asarray(v) for k, v in I.items()}
    ar = np.arange
    group = lambda n, w: [ar(a, a + w) for a in range(0, n, w)]
    store = {}
    place = [None] * NU
    hb = np.concatenate([ar(h * 64, h * 64 + 64) for h in HEADS_B])

    def put(i, a):
        u = UNITS[i]
        name = {"L": "wl", "M": "wm", "K": "wm"}[u["st"][0]] + f"_{a.shape[1]}"
        place[i] = len(store.setdefault(name, []))
        store[name].append(a)

    pos = 0
    for l in range(2):
        w = f["w_in"][l]
        order = [512 + hb[:256], 512 + hb[256:], ar(1024, 1280), ar(1280, 1536), ar(1536, 1792), ar(1792, 2048), ar(256, 512), ar(0, 256)]
        seq = _units_of(w, KD, order)
        wo = f["w_out"][l][np.concatenate([ar(256), 256 + hb, ar(768, 1024)])]
        seq += _units_of(wo, KD, group(D, 256))
        for h in range(2):
            seq += _units_of(f["w_up"][l], KD, [np.concatenate([ar(j * P, j * P + P), FF + ar(j * P, j * P + P)])
                                               for j in range(h * HALF, (h + 1) * HALF)])
            seq += _units_of(f["w_down"][l][h * HALF * P:(h + 1) * HALF * P], HALF, group(D, 128))
        for a in seq:
            put(pos, a)
            pos += 1
    seq = _units_of(f["lru_w_in_2"][0], KD, [np.concatenate([ar(j * P, j * P + P), LW + ar(j * P, j * P + P)]) for j in range(NL)])
    dense = []
    for name in ("lru_gate_a_w_2", "lru_gate_x_w_2"):
        m = np.zeros((LW, LW), np.float32)
        for b in range(LW // LB):
            m[b * LB:(b + 1) * LB, b * LB:(b + 1) * LB] = f[name][0, b]
        dense.append(m)
    for js in GATE_UNITS:
        seq.append(np.concatenate([dense[g][m * P:(m + 1) * P, j * P:(j + 1) * P] for j in js for g in range(2) for m in GATES[j]], axis=1))
    seq += _units_of(f["lru_w_out_2"][0], NL, group(D, 128))

    def mlp(l):
        out = []
        for h in range(2):
            out += _units_of(f["mlp_w1_2"][l], KD, [ar(h * 2048 + a, h * 2048 + a + 256) for a in range(0, 2048, 256)])
            out += _units_of(f["mlp_w2_2"][l][h * 2048:(h + 1) * 2048], 16, group(D, 128))
        return out

    seq += mlp(0) + _units_of(f["kv_w_2"], KD, group(2 * D, 256))
    seq += _units_of(f["attn_w_q_2"][0], KD, group(D, 256)) + _units_of(f["attn_w_o_2"][0], KD, group(D, 256)) + mlp(1)
    for a in seq:
        put(pos, a)
        pos += 1
    assert pos == NU
    ada, bada = [], []
    for w, b in ((f["w_ada"][0], f["b_ada"][0]), (f["w_ada"][1], f["b_ada"][1]), (f["ada_w_2"][0], f["ada_b_2"][0]),
                 (f["kv_ada_w_2"], f["kv_ada_b_2"]), (f["ada_w_2"][1], f["ada_b_2"][1])):
        ada += _units_of(w, 4, group(w.shape[1], 512))
        bada.append(b)
    col = lambda v: np.asarray(v).reshape(-1, P).T
    feat = np.concatenate(
        [col(np.concatenate(bada))]
        + [col(g) for g in (f["norm1_g"][0], f["norm2_g"][0], f["norm1_g"][1], f["norm2_g"][1], f["norm1_g_2"][0], f["norm2_g_2"][0],
                            f["kv_norm_g_2"], f["norm1_g_2"][1], f["norm2_g_2"][1])]
        + [col(f["conv_w"][:, :, 0, :]), col(f["conv_b"]), col(f["lru_conv_w_2"][0]), col(f["lru_conv_b_2"][0]),
           col(f["lru_gate_a_b_2"][0]), col(f["lru_gate_x_b_2"][0]), col(f["lru_lambda_2"][0]), col(f["c"]), col(f["c_ctx"]), col(f["c_2"])], axis=1)
    assert feat.shape[1] == NFEAT
    rows = []
    for l in range(2):
        rows += [f["b_qnorm"][l], f["b_knorm"][l], f["c_qnorm"][l], f["c_knorm"][l], f["c_lam"][l].ravel(), f["c_subln"][l], f["b_sink"][l][HEADS_B]]
    rows = np.concatenate(rows + [f["k_norm_g_2"], f["q_norm_g_2"][0]])
    assert rows.shape[0] == NROW
    x0 = np.concatenate([f["x"][0], f["ctx"][0]]).T.reshape(KD, P, 512).transpose(1, 0, 2).reshape(P, KD * 512)
    wsT = f["a_ws"].transpose(0, 3, 1, 2).reshape(2, P, 512)
    abs_ = f["a_bs"].reshape(2, 2, 2, P).transpose(0, 2, 1, 3).reshape(2, 2, 256)
    q, k = ar(128)[:, None] + 128, ar(256)[None, :]
    bias = f["rel_bias_2"][0][:, np.clip(q - k, -128, 128) + 128].transpose(1, 0, 2)
    out = {n: np.stack(v) for n, v in store.items()}
    out.update(ada=np.stack(ada), feat=feat, rows=rows, x0=x0, wsT=wsT, abs=abs_, bias=bias, cst=_constants())
    return {n: np.ascontiguousarray(v, np.float32) for n, v in out.items()}, place


def _constants():
    c = np.zeros((P, NCONST), np.float32)
    c[:, 0:128] = np.eye(P)
    c[:, 128:256] = 1.0
    p, j = np.arange(P)[:, None], np.arange(P)[None, :]
    c[:, 256:384] = np.where(j <= p, 0.0, NEG)
    c[:, 384:512] = np.where(j >= p, 0.0, NEG)
    tok = np.arange(SEQ)
    pos = np.stack([tok // 64, tok % 64], 1).astype(np.float32)
    for d, a, b in ((64, CONST["cb"], CONST["sb"]), (32, CONST["cc"], CONST["sc"])):
        f = d // 4
        inv = np.float32(10000.0) ** (-np.arange(f, dtype=np.float32) / np.float32(f))
        ang = (pos[:, :, None] * inv.astype(np.float32)).astype(np.float32)
        cos, sin = np.cos(ang), np.sin(ang)
        cs = np.stack([cos, cos], 2).reshape(2, P, d).transpose(1, 0, 2).reshape(P, 2 * d)
        sn = np.stack([-sin, sin], 2).reshape(2, P, d).transpose(1, 0, 2).reshape(P, 2 * d)
        c[:, a:a + 2 * d] = cs
        c[:, b:b + 2 * d] = sn
    return c


def write_program(nc, arrays, place, known):
    A = {n: nc.dram_tensor(f"in_{n}", a.shape, F32, kind="ExternalInput").ap() for n, a in arrays.items()}
    A["out"] = nc.dram_tensor("out_x", (P, KD, SEQ), F32, kind="ExternalOutput").ap()
    A["place"] = place
    return build(nc, A, known)


def kernel(**inputs):
    import concourse.bacc as bacc
    from concourse.bass_utils import run_bass_kernel_spmd
    arrays, place = _lay_out(inputs)
    counts = {}
    for _ in range(2):
        nc = bacc.Bacc("TRN2", target_bir_lowering=False, num_devices=1)
        counts = write_program(nc, arrays, place, counts)
    r = run_bass_kernel_spmd(nc, [{f"in_{n}": a for n, a in arrays.items()}], core_ids=[0])
    got = r.results[0]["out_x"]
    return np.ascontiguousarray(got.transpose(2, 1, 0).reshape(1, SEQ, D))
```

```python
from contextlib import ExitStack
import math

import numpy as np
import concourse.bass as bass
from concourse import mybir

F32 = mybir.dt.float32
F32R = mybir.dt.float32r
ALU = mybir.AluOpType
ACT = mybir.ActivationFunctionType
AX = mybir.AxisListType.X

P = 128
D = 1024
KD = D // P
SEQ = 256
CTX = 256
FF = 2816
NFF = FF // P
HALF = NFF // 2
LW = 1408
NL = LW // P
LB = 88
FF2 = 4096
EPS = 1e-6
NEG = -1e30
UMAX = 2048
RAW, SPLIT = 4, 3
AUXN = 3
HEADS_B = [0, 4, 1, 5, 2, 6, 3, 7]

ROWS = {}
_n = 0
for _l in range(2):
    for _name, _w in (("bq", 64), ("bk", 64), ("cq", 32), ("ck", 32), ("lam", 128), ("sub", 64), ("sink", 8)):
        ROWS[_name, _l] = (_n, _w)
        _n += _w
for _name in ("k2", "q2"):
    ROWS[_name, 0] = (_n, 64)
    _n += 64
NROW = _n
WARM_LEN = 4
MIX_SPLIT = 12
LT, LP, LO = 2, 3, 6
NVEC = 26
CTXV = 8
FEAT = {}
_n = 0
for _name, _w in (("bada", NVEC * 8), ("norm", 9 * 8), ("cw", 2 * 3 * 44), ("cb", 2 * 44), ("lcw", 4 * NL), ("lcb", NL),
                  ("lba", NL), ("lbx", NL), ("lam", NL), ("c", 24)):
    FEAT[_name] = _n
    _n += _w
NFEAT = _n
CONST = {"ident": 0, "ones": 128, "mask": 256, "cb": 512, "sb": 640, "cc": 768, "sc": 832}
NCONST = 896


def gate_tiles():
    out = []
    for j in range(NL):
        lo = (P * j) // LB * LB
        hi = min(-(-(P * (j + 1)) // LB) * LB, LW)
        out.append([m for m in range(NL) if P * m < hi and P * (m + 1) > lo])
    return out


GATES = gate_tiles()
GATE_UNITS = [list(range(a, min(a + 2, NL))) for a in range(0, NL, 2)]
MODTYPE = ["shift", "scale", "gate", "shift", "scale", "gate"]


def vec_base(stage):
    return {"L0": 0, "L1": 6, "M0": 12, "KV": 18, "M1": 20}[stage]


def make_units():
    u = []

    def add(kind, st, idx, kt, cols, T, **more):
        u.append(dict(kind=kind, st=st, idx=idx, kt=kt, cols=cols, T=T, i=len(u), **more))

    for l in range(2):
        T = 512 if l == 0 else 256
        st = f"L{l}"
        full, own = (4, 4) if l == 0 else (4, 2)
        for n, (name, nt) in enumerate([("cq", own), ("ck", full), ("av", own), ("au", own), ("bq0", own),
                                        ("bq1", own), ("bkv", full), ("cv", full)]):
            add(name, st, n, KD, 256, nt * 128, nt=nt)
        for n in range(4):
            add("out", st, n, KD, 256, T)
        for h in range(2):
            for n in range(HALF):
                add("up", st, h * HALF + n, KD, 256, T)
            for n in range(KD):
                add("down", st, h * KD + n, HALF, 128, T)
    for n in range(NL):
        add("lin", "M0", n, KD, 256, 256)
    for n in range(len(GATE_UNITS)):
        add("lgate", "M0", n, 2 * sum(len(GATES[j]) for j in GATE_UNITS[n]), 128, 256)
    for n in range(KD):
        add("lout", "M0", n, NL, 128, 256)

    def mlp(st):
        for h in range(2):
            for n in range(8):
                add("w1", st, h * 8 + n, KD, 256, 256)
            for n in range(KD):
                add("w2", st, h * KD + n, 16, 128, 256)

    mlp("M0")
    for n in range(8):
        add("k" if n < 4 else "v", "KV", n, KD, 256, 256, nt=2)
    for n in range(4):
        add("q", "M1", n, KD, 256, 256, nt=2)
    for n in range(4):
        add("out", "M1", n, KD, 256, 256)
    mlp("M1")
    return u


UNITS = make_units()
NU = len(UNITS)


def first_of(kind, st):
    return next(u["i"] for u in UNITS if u["kind"] == kind and u["st"] == st)


def make_program():
    prog = [("norm", 0, "L0", 512)]
    n = 1
    for st in ("L0", "L1", "M0", "KV", "M1"):
        for u in UNITS:
            if u["st"] != st:
                continue
            key = (u["kind"], u["idx"])
            if st in ("L0", "L1"):
                if key == ("out", 0):
                    prog.append(("attn", st))
                if key == ("up", 0):
                    prog.append(("norm", 1 + 2 * int(st[1]), st, 512 if st == "L0" else 256))
                if key == ("cq", 0) and st == "L1":
                    prog.append(("norm", 2, "L1", 512))
            if st == "M0":
                if key == ("lin", 0):
                    prog.append(("norm", 4, "M0", 256))
                if key == ("lgate", 0):
                    prog.append(("lsplit",))
                if key == ("lout", 0):
                    prog.append(("lscan",))
                if key == ("w1", 0):
                    prog.append(("norm", 5, "M0", 256))
            if key == ("k", 0):
                prog.append(("norm", 6, "KV", 256))
            if st == "M1":
                if key == ("q", 0):
                    prog.append(("norm", 7, "M1", 256))
                if key == ("out", 0):
                    prog.append(("attn", "M1"))
                if key == ("w1", 0):
                    prog.append(("norm", 8, "M1", 256))
            prog.append(("unit", u["i"]))
    return prog


PROGRAM = make_program()
FEEDS = {("out", "L0"): 1, ("down", "L0"): 2, ("out", "L1"): 3, ("down", "L1"): 4, ("lout", "M0"): 5,
         ("w2", "M0"): 6, ("out", "M1"): 8}
FIRST_HALF = {"down": KD, "w2": KD}


def fed_norm(u):
    n = FEEDS.get((u["kind"], u["st"]))
    if n is None or u["idx"] < FIRST_HALF.get(u["kind"], 0):
        return None
    return n


def chunks_of(u):
    if u["kind"] == "out":
        return [2 * u["idx"], 2 * u["idx"] + 1]
    return [u["idx"] % KD]


def ada_plan():
    n = [0] * NU
    n[0] = n[10] = 2
    for a, b, by in ((1, 7, 1), (8, 10, 1), (12, 50, 1), (52, 56, 1), (100, 111, 2), (117, 122, 1), (125, 163, 1)):
        for i in range(a, b, by):
            n[i] = 1
    n[53] = n[55] = n[6] = 0
    n[1] = 2
    left = NVEC * 4 - len(ADA_FIRST) - sum(n)
    assert -8 <= left <= 0, left
    for i in range(162, 162 + left, -1):
        n[i] = 0
    out, at = [], 8
    for i in range(NU):
        out.append(list(range(at, at + n[i])))
        at += n[i]
    assert at == NVEC * 4
    for st in ("L0", "L1", "M1"):
        assert sum(n[:first_of("out", st)]) % 2 == 0
    return out


ADA_FIRST = list(range(8))
ADA_AT = ada_plan()
REDUCE_AT = [[a // 2 for a in (ADA_AT[i - 1] if i else []) if a % 2] for i in range(NU)]


def raw_order():
    order = [("ada", a) for a in ADA_FIRST] + [("w", 0), ("w", 1)]
    for i in range(NU):
        if i + 2 < NU:
            order.append(("w", i + 2))
        order += [("ada", a) for a in ADA_AT[i]]
    return order


RAW_ORDER = raw_order()
RAW_AT = {key: n for n, key in enumerate(RAW_ORDER)}


def attention_tiles(st):
    out = []
    if st == "M1":
        for t in range(2):
            for hg in range(2):
                for s in range(8):
                    h = hg * 8 + s
                    out.append(dict(st=st, t=t, grp=("m", t, hg), slot=s, qc=h // 2, kc=h // 2, base=64 * (h % 2), K=64,
                                    k0=0, nk=128 * (t + 1), h=h, v=[(kt, 64 * h) for kt in range(t + 1)]))
        return out
    for kind in "cb":
        for t in range(4 if st == "L0" else 2):
            kts = [0, 1, 2, 3] if t < 2 else [2, 3]
            for s in range(8):
                x = dict(st=st, t=t, grp=(kind, t), slot=s, k0=128 * kts[0], nk=128 * len(kts))
                if kind == "b":
                    x.update(qc=s // 2, kc=4, base=64 * (s % 2), K=64, v=[(kt, 256 + 64 * (s % 2)) for kt in kts])
                else:
                    h, m = s // 2, s % 2
                    x.update(qc=5 + h // 2, kc=7 + h // 2, base=64 * (h % 2) + 32 * m, K=32, v=[(kt, 384 + 64 * h) for kt in kts])
                out.append(x)
    return out


class Counts:

    def __init__(self, known, sems):
        self.known, self.sems, self.seen, self.n = known, sems, {}, {}

    def tick(self, name, key, by=1):
        self.n[name] = self.n.get(name, 0) + by
        assert (name, key) not in self.seen, (name, key)
        self.seen[name, key] = self.n[name]
        self.last = self.sems[name], self.n[name]
        return self.sems[name], by

    def link(self, name):
        self.n[name] = self.n.get(name, 0) + 1
        self.last = self.sems[name], self.n[name]
        return self.sems[name], 1

    def has(self, name, key):
        return (name, key) in self.known

    def at(self, name, key):
        if not self.known:
            return self.sems[name], 1
        return self.sems[name], self.known[name, key]

    def note(self, name, key, value):
        self.seen[name, key] = value

    def noted(self, name, key):
        return self.known.get((name, key), 0)


SEMAPHORES = ["small", "x_in", "hi", "lo", "raw_used", "unit", "pm_act", "pm_dve", "aux", "aux_act", "aux_dve",
              "silu_c", "mod", "sq", "sumsq", "sd", "rinv", "xr", "hhi", "hlo", "xres",
              "zsq", "zss", "zsd", "z", "ztr", "vcopy", "gel", "avn", "mixm", "othi", "otlo",
              "negm", "p", "pt_act", "pt_dve", "ptr", "pv", "snk", "snkx", "o", "ocs", "ocss", "ocsd", "ocn",
              "cv1", "cvd", "silu", "prod", "ghi", "glo", "lg", "lx", "lxd", "lr", "la", "lm", "ls", "lh", "ly", "zn", "adap", "score", "sadd", "cstdma", "rowsdma", "mixdma", "biasdma",
              "act_chain", "dve_chain", "pool_chain", "outd", "prep", "prepa"]


def build(nc, A, known):
    with ExitStack() as stack:
        sems = {n: stack.enter_context(nc.semaphore("s_" + n)) for n in SEMAPHORES}
        raw_in = [stack.enter_context(nc.semaphore(f"s_raw{n}")) for n in range(RAW)]
        C = Counts(known, sems)
        tick, at = C.tick, C.at

        cursor = [16512]

        def sb(name, cols, dt=F32, offset=None):
            if offset is None:
                offset = cursor[0]
                cursor[0] += -(-cols * 4 // 32) * 32
            return nc.alloc_sbuf_tensor_at(name, [P, cols], dt, offset=offset)

        raw = sb("raw", RAW * UMAX)
        whi = sb("whi", SPLIT * UMAX, F32R)
        wlo = sb("wlo", SPLIT * UMAX, F32R)
        acc = sb("acc", 2 * 2 * 512)
        X = sb("X", KD * 512)
        Hhi = sb("Hhi", KD * 512, F32R)
        Hlo = sb("Hlo", KD * 512, F32R)
        T = sb("T", 4 * 512)
        reg0 = cursor[0]
        cursor[0] += 2 * HALF * 512 * 4
        Ghi = sb("Ghi", HALF * 512, F32R, reg0)
        Glo = sb("Glo", HALF * 512, F32R, reg0 + HALF * 512 * 4)
        zu = sb("zu", 2048, F32, reg0)
        QT = sb("QT", 9 * 512, F32, reg0 + 8192)
        vt = sb("vt", 4 * 640, F32, reg0 + 26624)
        ub = sb("ub", 1024, F32, reg0 + 36864)
        wsT = sb("wsT", 512, F32, reg0 + 40960)
        bsb = sb("bsb", 256, F32, reg0 + 43008)
        sqo = sb("sqo", 1024, F32, reg0 + 40960)
        GT = sb("GT", NL * 256, F32, reg0)
        XR = sb("XR", NL * 256, F32, reg0 + NL * 1024)
        LA = sb("LA", NL * 256, F32, reg0 + 2 * NL * 1024)
        LU = sb("LU", NL * 256, F32, reg0 + 3 * NL * 1024)
        KT2 = sb("KT2", 2048, F32, reg0)
        VT2 = sb("VT2", 2048, F32, reg0 + 8192)
        QT2 = sb("QT2", 2048, F32, reg0 + 16384)
        bias2 = sb("bias2", 4096, F32, reg0 + 24576)
        zu2 = sb("zu2", 1024, F32, reg0 + 40960)
        rows = sb("rows", NROW)
        feat = sb("feat", NFEAT)
        cst = sb("cst", NCONST)
        mod = sb("mod", NVEC * 16)
        silc = sb("silc", 24)
        lamt = sb("lamt", 2 * 8)
        lk = sb("lk", 6 * NL)
        st8 = sb("st8", 6 * 16)
        zst = sb("zst", 2 * 3 * 32)
        eps = sb("eps", 1)
        assert cursor[0] <= 229344, cursor[0]

        PM = stack.enter_context(nc.psum_tensor("PM", [P, 2, 1024], F32))
        PX = stack.enter_context(nc.psum_tensor("PX", [P, AUXN, 512], F32))
        PO = stack.enter_context(nc.psum_tensor("PO", [P, 512], F32))

        ident = cst[:, 0:128]
        ones = cst[:, 128:256]

        def fcol(name, n):
            return feat[:, FEAT[name] + n:FEAT[name] + n + 1]

        def row(name, l):
            a, w = ROWS[name, l]
            return rows[:, a:a + w]

        def modc(v, who, k):
            n = v * 16 + who * 8 + k
            return mod[:, n:n + 1]

        def slot_raw(n, size):
            return raw[:, (n % RAW) * UMAX:(n % RAW) * UMAX + size]

        def wslot(buf, i, size, off=0):
            a = (i % SPLIT) * UMAX + off
            return buf[:, a:a + size]

        def usize(u):
            return u["kt"] * u["cols"]

        def raw_ready(eng, key):
            n = RAW_AT[key]
            eng.wait_ge(raw_in[n % RAW], 16 * (n // RAW + 1))

        def pm(i, a, n):
            return PM[:, i % 2, a:a + n]

        def aux(key, a=0, n=512):
            b = C.noted("bank", key)
            return PX[:, b, a:a + n]

        def score(n, w):
            return PM[:, (n // 2) % 2, (n % 2) * 512:(n % 2) * 512 + w]

        def last_c(st):
            return max(n for n, x in enumerate(attention_tiles(st)) if x["grp"][0] == "c")

        def view(ap, pattern, **k):
            return ap.rearrange(pattern, **k)

        def bcast(ap, shape):
            return ap.to_broadcast(shape)

        def tslot(n, w=512):
            return T[:, n * 512:n * 512 + w]

        def heads(u):
            l = int(u["st"][1]) if u["st"][0] == "L" else 0
            return {"bq0": (64, 4, "bq", "b"), "bq1": (64, 4, "bq", "b"), "bkv": (64, 2, "bk", "b"), "cq": (32, 8, "cq", "c"),
                    "ck": (32, 8, "ck", "c"), "k": (64, 4, "k2", None), "q": (64, 4, "q2", None)}[u["kind"]] + (l,)

        def qk_halves(u):
            return {"bq0": [0, 1], "bq1": [2, 3], "bkv": [4], "cq": [5, 6], "ck": [7, 8]}.get(u["kind"]) or \
                [2 * u["idx"], 2 * u["idx"] + 1]

        def zbuf(u):
            n = u["i"] % 2
            if u["st"][0] == "L":
                return zu[:, n * 1024:n * 1024 + 256 * u["nt"]]
            return zu2[:, n * 512:n * 512 + 512]

        def is_qk(u):
            return u["kind"] in ("bq0", "bq1", "bkv", "cq", "ck", "k", "q")

        def hslot(k):
            return tslot((0, 1, 3)[k % 3])

        def rinv_of(n, W):
            return tslot(2) if W == 512 else X[:, 7 * 512 + 256:8 * 512]

        def moving(u):
            if u["kind"] in ("down", "w2"):
                return Ghi, Glo, u["T"]
            if u["st"] == "L1" and u["idx"] < 8 and u["kind"] not in ("out", "up", "down"):
                return Hhi, Hlo, 512
            return Hhi, Hlo, u["T"]

        def ptiles(st):
            base, w = (zu, 512) if st != "M1" else (zu2, 256)
            return [acc[:, n * 512:n * 512 + 512] for n in range(4)], [base[:, n * w:(n + 1) * w] for n in range(4)]

        def stat(what, g, a=0, n=8):
            o = what * 16 + (g % 2) * 8
            return st8[:, o + a:o + a + n]

        NEGM, DEN, SNK, REC = range(4)
        NTOK = {"L0": 4, "L1": 2, "M1": 2}
        groups = {}
        for s in ("L0", "L1", "M1"):
            for t in attention_tiles(s):
                groups.setdefault((s, t["grp"]), len(groups))

        block = stack.enter_context(nc.Block())

        @block.sync
        def _(sp):
            sp.dma_start(feat[:, :], A["feat"]).then_inc(*tick("small", "feat", 16))
            sp.dma_start(X[:, :], A["x0"]).then_inc(*tick("x_in", 0, 16))
            for n, (what, k) in enumerate(RAW_ORDER):
                if n >= RAW:
                    sp.wait_ge(*at("raw_used", n - RAW))
                if what == "ada":
                    src, size = A["ada"][k], UMAX
                else:
                    u = UNITS[k]
                    size = usize(u)
                    src = A[{"L": "wl", "M": "wm", "K": "wm"}[u["st"][0]] + f"_{size}"][A["place"][k]]
                sp.dma_start(slot_raw(n, size), src).then_inc(raw_in[n % RAW], 16)
            for c in range(KD):
                sp.wait_ge(*at("xres", ("M1", "last", c)))
                sp.dma_start(A["out"][:, c, :], X[:, c * 512:c * 512 + 256]).then_inc(*tick("outd", c, 16))
            sp.wait_ge(*at("outd", KD - 1))

        def pool_prod(pool, u):
            i, W = u["i"], u["T"]
            g, val = tslot(2 * (i % 2), W), tslot(2 * (i % 2) + 1, W)
            pool.wait_ge(*at("silu", i))
            pool.wait_ge(*at("cvd", (i, 1)))
            pool.tensor_tensor(g, g, val, ALU.mult).then_inc(*tick("prod", i))

        def rotate(pool, u):
            def link(ins):
                ins.then_inc(*C.link("pool_chain"))
                pool.wait_ge(*C.last)

            i = u["i"]
            d, g, gain, rot, l = heads(u)
            nt, w = u["nt"], (128 if u["kind"] == "bkv" else 256)
            z = zbuf(u)
            z4 = view(z, "p (t g d) -> p t g d", t=nt, d=d)
            pool.wait_ge(*at("pm_dve", i))
            g4 = row(gain, l).unsqueeze(1).unsqueeze(1).to_broadcast([P, nt, g, d])
            ins = pool.tensor_tensor(z4[:, :, 0:g, :], z4[:, :, 0:g, :], g4, ALU.mult)
            if rot is None:
                ins.then_inc(*tick("z", i))
                return
            link(ins)
            f = d // 4
            ct, stb = (CONST["cb"], CONST["sb"]) if rot == "b" else (CONST["cc"], CONST["sc"])
            sw = T[:, 1536:1536 + 2 * w]
            for t in range(2):
                zz = view(z[:, t * 256:t * 256 + w], "p (g a h f) -> p g a h f", a=2, h=2, f=f)
                ss = view(sw[:, t * w:(t + 1) * w], "p (g a h f) -> p g a h f", a=2, h=2, f=f)
                sn = view(cst[:, stb + t * d:stb + (t + 1) * d], "p (a h f) -> p a h f", a=2, h=2)
                for h in range(2):
                    pool.tensor_tensor(ss[:, :, :, h, :], zz[:, :, :, 1 - h, :],
                                      sn[:, :, h, :].unsqueeze(1).to_broadcast([P, g, 2, f]), ALU.mult)\
                        .then_inc(*C.link("pool_chain"))
            pool.wait_ge(*C.last)
            for t in range(2):
                zg = view(z[:, t * 256:t * 256 + w], "p (g d) -> p g d", d=d)
                ins = pool.tensor_tensor(zg, zg, cst[:, ct + t * d:ct + (t + 1) * d].unsqueeze(1).to_broadcast([P, g, d]), ALU.mult)
                ins.then_inc(*C.link("pool_chain"))
            pool.wait_ge(*C.last)
            zx = view(z[:, 0:512], "p (t c) -> p t c", t=2)[:, :, 0:w]
            pool.tensor_tensor(zx, zx, view(sw, "p (t c) -> p t c", t=2), ALU.add).then_inc(*tick("z", i))

        @block.gpsimd
        def _(pool):
            pool.dma_start(cst[:, :], A["cst"]).then_inc(*tick("cstdma", 0, 16))
            pool.dma_start(rows[:, :], bass.AP.partition_broadcast(A["rows"], P)).then_inc(*tick("rowsdma", 0, 16))

            def load_mix(l):
                pool.dma_start(wsT[:, :], A["wsT"][l]).then_inc(*tick("mixdma", ("wsT", l), 16))
                for hh in range(2):
                    src = A["abs"][l, hh]
                    pool.dma_start(bsb[64 * hh:64 * hh + 64, :], bass.AP.partition_broadcast(src, 64))\
                        .then_inc(*tick("mixdma", ("bs", l, hh), 16))

            load_mix(0)
            for step in PROGRAM:
                if step[0] == "norm":
                    _, n, st, W = step
                    if step[1] == 2:
                        pool.wait_ge(*at("unit", first_of("cq", "L1") - 1))
                        load_mix(1)
                    if n == 6:
                        pool.wait_ge(*at("unit", first_of("k", "KV") - 1))
                        src = A["bias"]
                        pool.dma_start(view(bias2[:, :], "p (h k) -> p h k", h=16), src).then_inc(*tick("biasdma", 0, 16))
                if step[0] == "unit":
                    u = UNITS[step[1]]
                    i = u["i"]
                    if u["kind"] == "up" and u["idx"] % HALF > 0:
                        pool_prod(pool, UNITS[i - 1])
                    if u["kind"] == "down" and u["idx"] % KD == 0:
                        pool_prod(pool, UNITS[i - 1])
                    if is_qk(u):
                        rotate(pool, u)
                if step[0] == "lscan":
                    for j in range(NL):
                        pool.wait_ge(*at("lh", j))
                        q = slice(j * 256, j * 256 + 256)
                        pool.tensor_tensor(LU[:, q], XR[:, q], GT[:, q], ALU.mult).then_inc(*tick("ly", j))

        @block.scalar
        def _(act):
            def link(ins):
                ins.then_inc(*C.link("act_chain"))
                act.wait_ge(*C.last)

            def split_hi(i):
                if i >= NU:
                    return
                u = UNITS[i]
                raw_ready(act, ("w", i))
                if i >= SPLIT:
                    act.wait_ge(*at("unit", i - SPLIT))
                act.activation(wslot(whi, i, usize(u)), slot_raw(RAW_AT["w", i], usize(u)), ACT.Copy)\
                    .then_inc(*tick("hi", i))

            def squares(n, chunks, W):
                for k in chunks:
                    if n:
                        act.wait_ge(*at("xres", (n, k)))
                    else:
                        act.wait_ge(*at("x_in", 0))
                    if k >= 2:
                        act.wait_ge(*at("sumsq", (n, k - 2)))
                    act.activation(tslot(2 + k % 2, W), X[:, k * 512:k * 512 + W], ACT.Square).then_inc(*tick("sq", (n, k)))

            act.wait_ge(*at("small", "feat"))
            act.activation(silc[:, :], feat[:, FEAT["c"]:FEAT["c"] + 24], ACT.Silu).then_inc(*tick("silu_c", 0))
            act.wait_ge(*at("prep", "lam"))
            act.activation(view(lamt[:, :], "p (l c) -> p l c", l=2)[:, :, 2:4], view(lamt[:, :], "p (l c) -> p l c", l=2)[:, :, 0:2],
                           ACT.Exp).then_inc(*tick("prepa", "lam"))
            act.wait_ge(*at("prep", "lru"))
            act.activation(lk[:, 2 * NL:3 * NL], lk[:, NL:2 * NL], ACT.Exp, scale=-1.0).then_inc(*tick("prepa", "lru"))
            squares(0, range(KD), 512)

            def ffn_stage2(u):
                i, W = u["i"], u["T"]
                g = tslot(2 * (i % 2), W)
                act.wait_ge(*at("cvd", (i, 0)))
                act.activation(g, g, ACT.Silu).then_inc(*tick("silu", i))

            def ffn_stage3(u):
                i, W = u["i"], u["T"]
                k = u["idx"] % HALF
                act.wait_ge(*at("prod", i))
                act.activation(Ghi[:, k * W:(k + 1) * W], tslot(2 * (i % 2), W), ACT.Copy).then_inc(*tick("ghi", i))

            def evac(u):
                i, W, kind = u["i"], u["T"], u["kind"]
                act.wait_ge(*C.last)
                if is_qk(u):
                    d, g, _, _, _ = heads(u)
                    nt, w = u["nt"], (128 if kind == "bkv" else 256)
                    act.wait_ge(*at("unit", i))
                    src = view(pm(i, 0, nt * 256), "p (t c) -> p t c", t=nt)
                    dst = view(T[:, 0:nt * w], "p (t c) -> p t c", t=nt)
                    act.activation(dst, src[:, :, 0:w], ACT.Square).then_inc(*tick("zsq", i))
                    if kind == "bkv":
                        act.activation(view(vt[:, :], "p (t c) -> p t c", t=4)[:, 0:nt, 256:384], src[:, :, 128:256], ACT.Copy)\
                            .then_inc(*tick("vcopy", i))
                    act.wait_ge(*at("zss", i))
                    n = nt * g
                    act.activation(zst[:, 32:32 + n], zst[:, 0:n], ACT.Sqrt, scale=1.0 / d, bias=eps[:, :]).then_inc(*tick("zsd", i))
                elif kind == "cv":
                    nt = u["nt"]
                    act.wait_ge(*at("unit", i))
                    act.activation(view(vt[:, :], "p (t c) -> p t c", t=4)[:, 0:nt, 384:640],
                                   view(pm(i, 0, nt * 256), "p (t c) -> p t c", t=nt), ACT.Copy).then_inc(*tick("pm_act", i))
                elif kind == "v":
                    n = u["idx"] - 4
                    act.wait_ge(*at("unit", i))
                    act.activation(view(VT2[:, :], "p (t c) -> p t c", t=2)[:, :, n * 256:n * 256 + 256],
                                   view(pm(i, 0, 512), "p (t c) -> p t c", t=2), ACT.Copy).then_inc(*tick("pm_act", i))
                elif kind == "av":
                    nt = u["nt"]
                    act.wait_ge(*at("unit", i))
                    v = view(vt[:, :], "p (t c) -> p t c", t=4)[:, 0:nt, 0:256]
                    act.activation(v, view(pm(i, 0, nt * 256), "p (t c) -> p t c", t=nt), ACT.Gelu_apprx_tanh)\
                        .then_inc(*tick("pm_act", i))
                    act.wait_ge(*at("pm_act", i))
                    act.activation(view(T[:, 0:nt * 256], "p (t c) -> p t c", t=nt), v, ACT.Square).then_inc(*tick("zsq", i))
                    act.wait_ge(*at("zss", i))
                    act.activation(zst[:, 32:32 + 4 * nt], zst[:, 0:4 * nt], ACT.Sqrt, scale=1.0 / 64, bias=eps[:, :])\
                        .then_inc(*tick("zsd", i))
                elif kind == "au":
                    act.wait_ge(*at("unit", i))
                    act.activation(view(ub[:, 0:2 * W], "p (c t) -> p c t", c=2), view(pm(i, 0, 1024), "p (c t) -> p c t", c=2)[:, :, 0:W],
                                   ACT.Gelu_apprx_tanh).then_inc(*tick("pm_act", i))
                elif kind == "up":
                    l, j = int(u["st"][1]), u["idx"]
                    act.wait_ge(*at("unit", i))
                    for part in range(2):
                        n = j + part * NFF
                        dst = tslot(2 * (i % 2) + part, W)
                        if u["idx"] % HALF > 1:
                            act.wait_ge(*at("glo", i - 2))
                        act.activation(dst, pm(i, part * 512, W), ACT.Identity, scale=fcol("cw", (l * 3 + 1) * 44 + n),
                                       bias=fcol("cb", l * 44 + n)).then_inc(*tick("cv1", (i, part)))
                elif kind == "lin":
                    j = u["idx"]
                    act.wait_ge(*at("unit", i))
                    act.activation(GT[:, j * 256:j * 256 + 256], pm(i, 0, 256), ACT.Gelu_apprx_tanh).then_inc(*tick("pm_act", i))
                    act.activation(XR[:, j * 256:j * 256 + 256], pm(i, 512, 256), ACT.Identity, scale=fcol("lcw", 3 * NL + j),
                                   bias=fcol("lcb", j)).then_inc(*tick("lx", j))
                elif kind == "lgate":
                    act.wait_ge(*at("unit", i))
                    js = GATE_UNITS[u["idx"]]
                    if u["idx"] >= 2:
                        act.wait_ge(*at("la", u["idx"] - 2))
                    rs = tslot(u["idx"] % 2)
                    for c, j in enumerate(js):
                        act.activation(rs[:, c * 256:c * 256 + 256], pm(i, c * 512, 256), ACT.Sigmoid, bias=fcol("lba", j))\
                            .then_inc(*C.link("act_chain"))
                    for c, j in enumerate(js):
                        ins = act.activation(LU[:, j * 256:j * 256 + 256], pm(i, c * 512 + 256, 256), ACT.Sigmoid, bias=fcol("lbx", j))
                        if c == len(js) - 1:
                            ins.then_inc(*tick("pm_act", i))
                            act.wait_ge(*at("pm_act", i))
                    for c, j in enumerate(js):
                        ins = act.activation(LA[:, j * 256:j * 256 + 256], rs[:, c * 256:c * 256 + 256], ACT.Tanh,
                                             scale=lk[:, 5 * NL + j:5 * NL + j + 1])
                    ins.then_inc(*tick("lr", u["idx"]))
                elif kind == "w1":
                    act.wait_ge(*at("unit", i))
                    r, g = tslot(2 * (i % 2)), tslot(2 * (i % 2) + 1)
                    if u["idx"] % 8 >= 2:
                        act.wait_ge(*at("glo", i - 2))
                    act.activation(view(r, "p (c t) -> p c t", c=2), view(pm(i, 0, 1024), "p (c t) -> p c t", c=2)[:, :, 0:256],
                                   ACT.Relu).then_inc(*tick("pm_act", i))
                    act.wait_ge(*at("pm_act", i))
                    act.activation(g, r, ACT.Square).then_inc(*tick("silu", i))
                    act.wait_ge(*at("silu", i))
                    k = u["idx"] % 8
                    act.activation(Ghi[:, k * 512:k * 512 + 512], g, ACT.Copy).then_inc(*tick("ghi", i))
                n = fed_norm(u)
                if n is not None:
                    squares(n, chunks_of(u), 512 if u["st"] == "L0" or n == 2 else 256)

            def attn(st):
                tiles = attention_tiles(st)
                Ps, PTs = ptiles(st)
                nt = NTOK[st]
                def finish_c():
                    act.wait_ge(*at("ocss", st))
                    act.activation(zst[:, 32:32 + 4 * nt], zst[:, 0:4 * nt], ACT.Sqrt, scale=1.0 / 64, bias=eps[:, :])\
                        .then_inc(*tick("ocsd", st))
                    W = 128 * nt
                    for tp in range(nt // 2):
                        key = ("OC", st, tp)
                        act.wait_ge(*at("aux", key))
                        dst = view(Hhi[:, 6 * W:8 * W], "p (c t) -> p c t", c=2)[:, :, tp * 256:tp * 256 + 256]
                        act.activation(dst, view(aux(key), "p (c t) -> p c t", c=2), ACT.Copy).then_inc(*tick("othi", key))

                for n in range(len(tiles) + LO):
                    if st != "M1" and n == MIX_SPLIT:
                        act.wait_ge(*at("mixm", (st, 1, nt // 2 - 1)))
                        act.wait_ge(*at("unit", first_of("out", st) - 1))
                        act.activation(Hhi[:, 0:256 * nt], ub[:, 0:256 * nt], ACT.Copy).then_inc(*tick("othi", (st, "a")))
                    if n < len(tiles):
                        x = tiles[n]
                        g = groups[st, x["grp"]]
                        act.wait_ge(*at("negm", (st, n)))
                        if n >= 4:
                            act.wait_ge(*at("aux", ("T", st, n - 4)))
                        dst = Ps[n % 4][:, 0:x["nk"]]
                        src = dst if st == "M1" else score(n, x["nk"])
                        act.activation(dst, src, ACT.Exp, bias=stat(NEGM, g, x["slot"], 1),
                                       accum_out=stat(DEN, g, x["slot"], 1)).then_inc(*tick("p", (st, n)))
                        if x["slot"] == 7 and x["grp"][0] == "b":
                            act.wait_ge(*at("snk", (st, n)))
                            act.activation(stat(SNK, g), stat(SNK, g), ACT.Exp).then_inc(*tick("snkx", (st, n)))
                    m = n - LT
                    if 0 <= m < len(tiles) and m % 2 == 0:
                        x = tiles[m]
                        act.wait_ge(*at("aux", ("T", st, m)))
                        if m >= 4:
                            act.wait_ge(*at("pv", (st, m - 4)))
                        act.activation(PTs[m % 4][:, 0:x["nk"]], aux(("T", st, m), 0, x["nk"]), ACT.Copy)\
                            .then_inc(*tick("aux_act", ("T", st, m)))
                    m = n - LO
                    if m >= 0 and tiles[m]["slot"] == 7 and tiles[m]["grp"][0] != "c":
                        x = tiles[m]
                        key = ("OT", st, x["grp"])
                        act.wait_ge(*at("aux", key))
                        c0 = 2 if st != "M1" else 4 * x["grp"][2]
                        W = 128 * nt
                        dst = view(Hhi[:, c0 * W:(c0 + 4) * W], "p (c t) -> p c t", c=4)[:, :, x["t"] * 128:x["t"] * 128 + 128]
                        act.activation(dst, view(aux(key), "p (c t) -> p c t", c=4), ACT.Copy).then_inc(*tick("othi", key))
                    if st != "M1" and n == last_c(st) + LO:
                        finish_c()

            def root(n, W):
                act.wait_ge(*at("sumsq", (n, 7)))
                act.activation(rinv_of(n, W), PO[:, 0:W], ACT.Sqrt, scale=1.0 / D, bias=eps[:, :]).then_inc(*tick("sd", n))

            act.wait_ge(*at("prep", "eps"))
            root(0, 512)
            for i in range(2):
                split_hi(i)
            for step in PROGRAM:
                if step[0] == "norm":
                    _, n, st, W = step
                    if n not in (0, 7):
                        root(n, W)
                    v = vec_base(st) + (3 if n in (1, 3, 5, 8) else 0)
                    for k in range(KD):
                        act.wait_ge(*at("xr", (n, k)))
                        for who in range(W // 256):
                            o = k * W + who * 256
                            ins = act.activation(Hhi[:, o:o + 256], hslot(k)[:, who * 256:who * 256 + 256], ACT.Identity,
                                                 bias=modc(v, who, k))
                        ins.then_inc(*tick("hhi", (n, k)))
                elif step[0] == "attn":
                    prev = UNITS[first_of("out", step[1]) - 1]
                    attn(step[1])
                elif step[0] == "lsplit":
                    act.wait_ge(*at("unit", first_of("lgate", "M0") - 1))
                    for j in range(NL):
                        act.wait_ge(*at("lxd", j))
                        act.activation(Hhi[:, j * 256:j * 256 + 256], XR[:, j * 256:j * 256 + 256], ACT.Copy).then_inc(*tick("hhi", ("x", j)))
                elif step[0] == "lscan":
                    act.wait_ge(*at("lm", 0))
                    for h in range(2):
                        q = slice(h * 6 * 256, min((h + 1) * 6, NL) * 256)
                        act.activation(XR[:, q], XR[:, q], ACT.Sqrt, scale=-1.0).then_inc(*tick("ls", h))
                    for j in range(NL):
                        act.wait_ge(*at("ly", j))
                        act.activation(Hhi[:, j * 256:j * 256 + 256], LU[:, j * 256:j * 256 + 256], ACT.Copy).then_inc(*tick("hhi", ("y", j)))
                else:
                    u = UNITS[step[1]]
                    i = u["i"]
                    up_before = u["kind"] in ("up", "down") and UNITS[i - 1]["kind"] == "up"
                    if up_before:
                        ffn_stage2(UNITS[i - 1])
                    split_hi(i + 2)
                    if up_before:
                        ffn_stage3(UNITS[i - 1])
                    evac(u)

        @block.vector
        def _(dve):
            def link(ins):
                ins.then_inc(*C.link("dve_chain"))
                dve.wait_ge(*C.last)

            def split_lo(i):
                if i >= NU:
                    return
                u = UNITS[i]
                dve.wait_ge(*at("hi", i))
                n = RAW_AT["w", i]
                dve.tensor_tensor(wslot(wlo, i, usize(u)), slot_raw(n, usize(u)), wslot(whi, i, usize(u)).bitcast(F32), ALU.subtract)\
                    .then_inc(*tick("raw_used", n))

            marks = [None, None]

            def ada(a):
                hv, part = a // 2, a % 2
                v = hv // 2
                who_c = 0 if v < 12 else 2
                n = RAW_AT["ada", a]
                raw_ready(dve, ("ada", a))
                if part == 0 and hv >= 2:
                    dve.wait_ge(*at("aux", ("ada", hv - 2)))
                two = v < CTXV
                if two or part == 0:
                    dve.wait_ge(*C.last)
                for k in range(4):
                    w = slot_raw(n, UMAX)[:, k * 512:k * 512 + 512]
                    kk = part * 4 + k
                    for who in range(2 if two else 1):
                        s = silc[:, (who_c + who) * 8 + kk:(who_c + who) * 8 + kk + 1]
                        half = who if two else k % 2
                        dst = acc[:, (hv % 2) * 1024 + half * 512:(hv % 2) * 1024 + half * 512 + 512]
                        if kk < (1 if two else 2):
                            ins = dve.tensor_scalar(dst, w, s, None, ALU.mult)
                        else:
                            dve.wait_ge(*marks[half])
                            ins = dve.scalar_tensor_tensor(out=dst, in0=w, scalar=s, in1=dst, op0=ALU.mult, op1=ALU.add)
                        if k == 3 and who == (1 if two else 0):
                            ins.then_inc(*tick("raw_used", n))
                        else:
                            ins.then_inc(*C.link("dve_chain"))
                        marks[half] = C.last

            def ada_done(hv):
                v, half = hv // 2, hv % 2
                key = ("ada", hv)
                dve.wait_ge(*at("aux", key))
                nw = 2 if v < CTXV else 1
                base = {0: 0, 1: 6, 2: 12, 3: 18, 4: 20}[0 if v < 6 else 1 if v < 12 else 2 if v < 18 else 3 if v < 20 else 4]
                kind = MODTYPE[v - base]
                dst = view(mod[:, v * 16:v * 16 + 16], "p (w k) -> p w k", w=2)[:, 0:nw, half * 4:half * 4 + 4]
                order = "p (k w) -> p w k" if hv < 4 else "p (w k) -> p w k"
                srcv = view(aux(key, 0, 8), order, w=2)[:, 0:nw, :]
                bia = feat[:, FEAT["bada"] + v * 8 + half * 4:FEAT["bada"] + v * 8 + half * 4 + 4].unsqueeze(1).to_broadcast([P, nw, 4])
                ins = dve.tensor_tensor(dst, srcv, bia, ALU.add)
                if kind == "scale":
                    norm = {1: 0, 4: 1, 7: 2, 10: 3, 13: 4, 16: 5, 19: 6, 21: 7, 24: 8}[v]
                    ins.then_inc(*tick("aux_dve", key))
                    dve.wait_ge(*at("aux_dve", key))
                    g = feat[:, FEAT["norm"] + norm * 8 + half * 4:FEAT["norm"] + norm * 8 + half * 4 + 4].unsqueeze(1).to_broadcast([P, nw, 4])
                    ins = dve.scalar_tensor_tensor(out=dst, in0=dst, scalar=1.0, in1=g, op0=ALU.add, op1=ALU.mult)
                    ins.then_inc(*tick("mod", v if half else ("half", v)))
                else:
                    ins.then_inc(*tick("aux_dve", key))

            def mod_ready(v):
                return at("aux_dve", ("ada", 2 * v + 1))

            dve.memset(eps[:, :], EPS).then_inc(*tick("prep", "eps"))
            dve.wait_ge(*at("rowsdma", 0))
            dve.wait_ge(*at("cstdma", 0))
            for l in range(2):
                lam = view(row("lam", l), "p (a b d) -> p a b d", a=2, b=2)
                link(dve.tensor_tensor(view(T[:, l * 64:l * 64 + 64], "p (a d) -> p a d", a=2), lam[:, :, 0, :], lam[:, :, 1, :], ALU.mult))
                ins = dve.reduce_sum(lamt[:, l * 8:l * 8 + 2], view(T[:, l * 64:l * 64 + 64], "p (a d) -> p a d", a=2), AX)
                if l == 0:
                    link(ins)
                else:
                    ins.then_inc(*tick("prep", "lam"))
                link(dve.tensor_scalar(row("bq", l), row("bq", l), 64 ** -0.5, None, ALU.mult))
                link(dve.tensor_scalar(row("cq", l), row("cq", l), 32 ** -0.5, None, ALU.mult))
                init = 0.8 - 0.6 * math.exp(-0.3 * l)
                link(dve.tensor_scalar(row("sub", l), row("sub", l), 1.0 - init, None, ALU.mult))
            link(dve.tensor_scalar(row("q2", 0), row("q2", 0), 64 ** -0.5, None, ALU.mult))
            dve.wait_ge(*at("prepa", "lam"))
            for l in range(2):
                init = 0.8 - 0.6 * math.exp(-0.3 * l)
                link(dve.tensor_tensor(lamt[:, l * 8 + 4:l * 8 + 5], lamt[:, l * 8 + 2:l * 8 + 3], lamt[:, l * 8 + 3:l * 8 + 4], ALU.subtract))
                link(dve.tensor_scalar(lamt[:, l * 8 + 5:l * 8 + 6], lamt[:, l * 8 + 4:l * 8 + 5], init, None, ALU.add))
            dve.wait_ge(*at("small", "feat"))
            lamf = feat[:, FEAT["lam"]:FEAT["lam"] + NL]
            neg, ab, e, w, w2, res = (lk[:, a * NL:(a + 1) * NL] for a in range(6))
            link(dve.tensor_scalar(neg, lamf, -1.0, None, ALU.mult))
            dve.tensor_tensor(ab, neg, lamf, ALU.max).then_inc(*tick("prep", "lru"))
            dve.wait_ge(*at("prepa", "lru"))
            link(dve.tensor_scalar(w2, e, 2.0, None, ALU.add))
            link(dve.reciprocal(res, w2))
            link(dve.tensor_tensor(w, e, res, ALU.mult))
            link(dve.tensor_tensor(w2, w, w, ALU.mult))
            link(dve.tensor_scalar(res, w2, 1.0 / 19, 1.0 / 17, ALU.mult, ALU.add))
            for m in range(7, -1, -1):
                link(dve.tensor_tensor(res, res, w2, ALU.mult))
                link(dve.tensor_scalar(res, res, 1.0 / (2 * m + 1), None, ALU.add))
            link(dve.tensor_tensor(res, res, w, ALU.mult))
            link(dve.tensor_scalar(neg, neg, 0.0, 4.0, ALU.max, ALU.mult))
            link(dve.scalar_tensor_tensor(out=res, in0=res, scalar=8.0, in1=neg, op0=ALU.mult, op1=ALU.add))

            def head_norm(u):
                i = u["i"]
                d, g, gain, rot, l = heads(u)
                nt, w = u["nt"], (128 if u["kind"] == "bkv" else 256)
                n = nt * g
                dve.wait_ge(*at("zsq", i))
                dve.reduce_sum(zst[:, 0:n], view(T[:, 0:nt * w], "p (g d) -> p g d", d=d), AX).then_inc(*tick("zss", i))
                dve.wait_ge(*at("zsd", i))
                link(dve.reciprocal(zst[:, 64:64 + n], zst[:, 32:32 + n]))
                z = zbuf(u)
                if i >= 2 and is_qk(UNITS[i - 2]):
                    for h in range(len(qk_halves(UNITS[i - 2]))):
                        dve.wait_ge(*at("aux", ("qkT", i - 2, h)))
                z4 = view(z, "p (t g d) -> p t g d", t=nt, d=d)
                src4 = view(pm(i, 0, nt * 256), "p (t g d) -> p t g d", t=nt, d=d)
                r4 = view(zst[:, 64:64 + n], "p (t g) -> p t g", t=nt).unsqueeze(3).to_broadcast([P, nt, g, d])
                dve.tensor_tensor(z4[:, :, 0:g, :], src4[:, :, 0:g, :], r4, ALU.mult).then_inc(*tick("pm_dve", i))

            def qk_copy(u):
                i, nt = u["i"], u["nt"]
                for h, c in enumerate(qk_halves(u)):
                    key = ("qkT", i, h)
                    dve.wait_ge(*at("aux", key))
                    if u["st"][0] == "L":
                        dst = QT[:, c * 512:c * 512 + nt * 128]
                    else:
                        dst = (KT2 if u["kind"] == "k" else QT2)[:, c * 256:c * 256 + 256]
                    dve.tensor_copy(dst, aux(key, 0, nt * 128)).then_inc(*tick("aux_dve", key))

            def residual(u):
                i, W = u["i"], u["T"]
                st = u["st"]
                v = vec_base(st) + (2 if u["kind"] in ("out", "lout") else 5)
                n = fed_norm(u)
                final = u["kind"] == "w2" and st == "M1" and u["idx"] >= KD
                dve.wait_ge(*at("unit", i))
                dve.wait_ge(*mod_ready(v))
                cs = chunks_of(u)
                for m, c in enumerate(cs):
                    for who in range(W // 256):
                        dst = X[:, c * 512 + who * 256:c * 512 + who * 256 + 256]
                        ins = dve.scalar_tensor_tensor(out=dst, in0=pm(i, m * 512 + who * 256, 256), scalar=modc(v, who, c),
                                                       in1=dst, op0=ALU.mult, op1=ALU.add)
                        lastw = who == W // 256 - 1
                        if lastw and n is not None:
                            ins.then_inc(*tick("xres", (n, c)))
                        elif lastw and final:
                            ins.then_inc(*tick("xres", (st, "last", c)))
                        elif lastw and m == len(cs) - 1:
                            ins.then_inc(*tick("pm_dve", i))
                            dve.wait_ge(*at("pm_dve", i))

            def evac(u):
                i, W, kind = u["i"], u["T"], u["kind"]
                dve.wait_ge(*C.last)
                if is_qk(u):
                    head_norm(u)
                elif kind == "av":
                    nt = u["nt"]
                    dve.wait_ge(*at("zsq", i))
                    dve.reduce_sum(zst[:, 0:4 * nt], view(T[:, 0:nt * 256], "p (g d) -> p g d", d=64), AX).then_inc(*tick("zss", i))
                    dve.wait_ge(*at("zsd", i))
                    link(dve.reciprocal(zst[:, 64:64 + 4 * nt], zst[:, 32:32 + 4 * nt]))
                    v4 = view(view(vt[:, :], "p (t c) -> p t c", t=4)[:, 0:nt, 0:256], "p t (g d) -> p t g d", d=64)
                    r4 = view(zst[:, 64:64 + 4 * nt], "p (t g) -> p t g", t=nt).unsqueeze(3).to_broadcast([P, nt, 4, 64])
                    dve.tensor_tensor(v4, v4, r4, ALU.mult).then_inc(*tick("avn", i))
                elif kind in ("out", "down", "lout", "w2"):
                    residual(u)
                    return
                elif kind == "up":
                    l, j = int(u["st"][1]), u["idx"]
                    ns = W // 256
                    for part in range(2):
                        n = j + part * NFF
                        dve.wait_ge(*at("cv1", (i, part)))
                        ps = view(pm(i, part * 512, W), "p (s t) -> p s t", s=ns)
                        y = view(tslot(2 * (i % 2) + part, W), "p (s t) -> p s t", s=ns)
                        link(dve.scalar_tensor_tensor(out=y[:, :, 1:256], in0=ps[:, :, 0:255], scalar=fcol("cw", (l * 3 + 0) * 44 + n),
                                                      in1=y[:, :, 1:256], op0=ALU.mult, op1=ALU.add))
                        dve.scalar_tensor_tensor(out=y[:, :, 0:255], in0=ps[:, :, 1:256], scalar=fcol("cw", (l * 3 + 2) * 44 + n),
                                                 in1=y[:, :, 0:255], op0=ALU.mult, op1=ALU.add).then_inc(*tick("cvd", (i, part)))
                elif kind == "lin":
                    j = u["idx"]
                    dve.wait_ge(*at("lx", j))
                    for s in range(1, 4):
                        y = XR[:, j * 256 + s:j * 256 + 256]
                        ins = dve.scalar_tensor_tensor(out=y, in0=pm(i, 512, 256 - s), scalar=fcol("lcw", (3 - s) * NL + j), in1=y,
                                                       op0=ALU.mult, op1=ALU.add)
                        if s < 3:
                            link(ins)
                        else:
                            ins.then_inc(*tick("lxd", j))
                elif kind == "lgate":
                    js = GATE_UNITS[u["idx"]]
                    w = 256 * len(js)
                    dve.wait_ge(*at("lr", u["idx"]))
                    s = tslot(2 + u["idx"] % 2, w)
                    th, u_, x_ = (b[:, js[0] * 256:js[0] * 256 + w] for b in (LA, LU, XR))
                    link(dve.tensor_scalar(s, th, 1.0, None, ALU.add))
                    link(dve.reciprocal(s, s))
                    link(dve.scalar_tensor_tensor(out=s, in0=s, scalar=2.0, in1=th, op0=ALU.mult, op1=ALU.mult))
                    dve.tensor_scalar(th, s, -1.0, 1.0, ALU.mult, ALU.add).then_inc(*C.link("dve_chain"))
                    link(dve.tensor_tensor(u_, u_, x_, ALU.mult))
                    dve.scalar_tensor_tensor(out=x_, in0=s, scalar=2.0, in1=s, op0=ALU.subtract, op1=ALU.mult).then_inc(*tick("la", u["idx"]))
                elif kind == "w1":
                    dve.wait_ge(*at("ghi", i))
                    k = u["idx"] % 8
                    dve.tensor_tensor(Glo[:, k * 512:k * 512 + 512], tslot(2 * (i % 2) + 1), Ghi[:, k * 512:k * 512 + 512].bitcast(F32),
                                      ALU.subtract).then_inc(*tick("glo", i))

            def ffn_lo(u):
                i, W = u["i"], u["T"]
                k = u["idx"] % HALF
                dve.wait_ge(*at("ghi", i))
                dve.tensor_tensor(Glo[:, k * W:(k + 1) * W], tslot(2 * (i % 2), W), Ghi[:, k * W:(k + 1) * W].bitcast(F32), ALU.subtract)\
                    .then_inc(*tick("glo", i))

            def mix(st):
                nt = NTOK[st]
                W = 128 * nt
                dve.wait_ge(*at("mixdma", ("bs", int(st[1]), 1)))
                dve.wait_ge(*at("pm_act", first_of("au", st)))
                for j in range(2):
                    for tp in range(nt // 2):
                        key = ("mix", st, j, tp)
                        dve.wait_ge(*C.last)
                        dve.wait_ge(*at("aux", key))
                        o = 1024 + (j * 2 + tp) % 2 * 256
                        m = T[:, o:o + 256]
                        for hh in range(2):
                            q = slice(64 * hh, 64 * hh + 64)
                            src = PX[q, C.noted("bank", key), :].rearrange("p (t g c) -> p t g c", t=2, g=2)[:, :, hh, :]
                            bs = bsb[q, j * 128:j * 128 + 128].unsqueeze(1).to_broadcast([64, 2, 128])
                            mm = m[q, :].rearrange("p (t c) -> p t c", t=2)
                            dve.tensor_tensor(mm, src, bs, ALU.add).then_inc(*(tick("aux_dve", key) if hh else C.link("dve_chain")))
                        dve.wait_ge(*C.last)
                        gate = ub[:, j * W + tp * 256:j * W + tp * 256 + 256]
                        dve.tensor_tensor(gate, m, gate, ALU.mult).then_inc(*tick("mixm", (st, j, tp)))

            def attn(st):
                tiles = attention_tiles(st)
                Ps, PTs = ptiles(st)
                nt = NTOK[st]
                W = 128 * nt
                def finish_c():
                    l = int(st[1])
                    oc = T[:, 1024:1024 + 256 * nt]
                    link(dve.tensor_tensor(sqo[:, 0:256 * nt], oc, oc, ALU.mult))
                    dve.reduce_sum(zst[:, 0:4 * nt], view(sqo[:, 0:256 * nt], "p (g d) -> p g d", d=64), AX).then_inc(*tick("ocss", st))
                    dve.wait_ge(*at("ocsd", st))
                    link(dve.reciprocal(zst[:, 64:64 + 4 * nt], zst[:, 32:32 + 4 * nt]))
                    oc = view(oc, "p (g d) -> p g d", d=64)
                    link(dve.tensor_tensor(oc, oc, zst[:, 64:64 + 4 * nt].unsqueeze(2).to_broadcast([P, 4 * nt, 64]), ALU.mult))
                    dve.tensor_tensor(oc, oc, row("sub", l).unsqueeze(1).to_broadcast([P, 4 * nt, 64]), ALU.mult).then_inc(*tick("ocn", st))
                    for tp in range(nt // 2):
                        key = ("OC", st, tp)
                        dve.wait_ge(*at("othi", key))
                        dst, hi = (view(b[:, 6 * W:8 * W], "p (c t) -> p c t", c=2)[:, :, tp * 256:tp * 256 + 256] for b in (Hlo, Hhi))
                        dve.tensor_tensor(dst, view(aux(key), "p (c t) -> p c t", c=2), hi.bitcast(F32), ALU.subtract)\
                            .then_inc(*tick("aux_dve", key))

                dve.wait_ge(*C.last)
                for n in range(len(tiles) + LO):
                    if n < len(tiles):
                        x = tiles[n]
                        g, s = groups[st, x["grp"]], x["slot"]
                        dve.wait_ge(*at("score", (st, n)))
                        src = score(n, x["nk"])
                        if st == "M1":
                            if n >= 4:
                                dve.wait_ge(*at("aux", ("T", st, n - 4)))
                            p = Ps[n % 4][:, 0:x["nk"]]
                            dve.wait_ge(*at("biasdma", 0))
                            b = bias2[:, x["h"] * 256 + 256 - x["nk"]:x["h"] * 256 + 256]
                            dve.tensor_tensor(p, src, b, ALU.add).then_inc(*tick("sadd", (st, n)))
                            dve.wait_ge(*at("sadd", (st, n)))
                            link(dve.memset(p[0:64, x["nk"] - 64:x["nk"]], NEG))
                            dve.tensor_reduce(stat(NEGM, g, s, 1), p, AX, ALU.max, negate=True).then_inc(*tick("negm", (st, n)))
                        elif x["grp"][0] == "b":
                            link(dve.tensor_reduce(stat(REC, g, s, 1), src, AX, ALU.max))
                            sk = row("sink", int(st[1]))[:, s:s + 1]
                            dve.tensor_scalar(stat(NEGM, g, s, 1), stat(REC, g, s, 1), sk, -1.0, ALU.max, ALU.mult)\
                                .then_inc(*tick("negm", (st, n)))
                            if s == 7:
                                dve.wait_ge(*at("negm", (st, n)))
                                dve.tensor_tensor(stat(SNK, g), stat(NEGM, g), row("sink", int(st[1])), ALU.add).then_inc(*tick("snk", (st, n)))
                        else:
                            dve.tensor_reduce(stat(NEGM, g, s, 1), src, AX, ALU.max, negate=True).then_inc(*tick("negm", (st, n)))
                    m = n - LT
                    if 0 <= m < len(tiles) and m % 2 == 1:
                        x = tiles[m]
                        dve.wait_ge(*at("aux", ("T", st, m)))
                        if m >= 4:
                            dve.wait_ge(*at("pv", (st, m - 4)))
                        dve.tensor_copy(PTs[m % 4][:, 0:x["nk"]], aux(("T", st, m), 0, x["nk"]))\
                            .then_inc(*tick("aux_dve", ("T", st, m)))
                    m = n - LP
                    if 0 <= m < len(tiles) and tiles[m]["slot"] == 7:
                        x = tiles[m]
                        grp = x["grp"]
                        g = groups[st, grp]
                        dve.wait_ge(*at("p", (st, m)))
                        if grp[0] == "b":
                            dve.wait_ge(*at("snkx", (st, m)))
                            link(dve.tensor_tensor(stat(DEN, g), stat(DEN, g), stat(SNK, g), ALU.add))
                        link(dve.reciprocal(stat(REC, g), stat(DEN, g)))
                        if grp[0] == "c":
                            odd = view(stat(REC, g), "p (h m) -> p h m", m=2)[:, :, 1]
                            link(dve.tensor_scalar(odd, odd, lamt[:, int(st[1]) * 8 + 5:int(st[1]) * 8 + 6], None, ALU.mult))
                        dve.wait_ge(*at("pv", (st, m)))
                        ob = tslot(g % 2)
                        prev = [k for k, v in groups.items() if v == g - 2 and k[0] == st]
                        if prev and prev[0][1][0] != "c":
                            dve.wait_ge(*at("aux", ("OT", st, prev[0][1])))
                        dve.tensor_tensor(view(ob, "p (s d) -> p s d", s=8), view(PO[:, :], "p (s d) -> p s d", s=8),
                                          stat(REC, g).unsqueeze(2).to_broadcast([P, 8, 64]), ALU.mult)\
                            .then_inc(*tick("pm_dve", ("PO", st, grp)))
                        if grp[0] == "c":
                            dve.wait_ge(*at("pm_dve", ("PO", st, grp)))
                            o4 = view(ob, "p (h m d) -> p h m d", h=4, m=2)
                            oc = view(T[:, 1024 + x["t"] * 256:1024 + x["t"] * 256 + 256], "p (h d) -> p h d", h=4)
                            dve.tensor_tensor(oc, o4[:, :, 0, :], o4[:, :, 1, :], ALU.subtract).then_inc(*tick("o", (st, grp)))
                            dve.wait_ge(*C.last)
                    m = n - LO
                    if m >= 0 and tiles[m]["slot"] == 7 and tiles[m]["grp"][0] != "c":
                        x = tiles[m]
                        key = ("OT", st, x["grp"])
                        dve.wait_ge(*at("othi", key))
                        c0 = 2 if st != "M1" else 4 * x["grp"][2]
                        dst, hi = (view(b[:, c0 * W:(c0 + 4) * W], "p (c t) -> p c t", c=4)[:, :, x["t"] * 128:x["t"] * 128 + 128]
                                   for b in (Hlo, Hhi))
                        dve.tensor_tensor(dst, view(aux(key), "p (c t) -> p c t", c=4), hi.bitcast(F32), ALU.subtract)\
                            .then_inc(*tick("aux_dve", key))
                    if st != "M1" and n == last_c(st) + LO:
                        finish_c()
                    if st != "M1" and n == MIX_SPLIT:
                        dve.wait_ge(*at("othi", (st, "a")))
                        dve.tensor_tensor(Hlo[:, 0:256 * nt], ub[:, 0:256 * nt], Hhi[:, 0:256 * nt].bitcast(F32), ALU.subtract)\
                            .then_inc(*tick("otlo", (st, "a")))

            def scan_lo(j):
                q = slice(j * 256, j * 256 + 256)
                dve.wait_ge(*at("hhi", ("y", j)))
                dve.tensor_tensor(Hlo[:, q], LU[:, q], Hhi[:, q].bitcast(F32), ALU.subtract).then_inc(*tick("hlo", ("y", j)))

            dve.wait_ge(*at("sd", 0))
            dve.reciprocal(rinv_of(0, 512), rinv_of(0, 512)).then_inc(*tick("rinv", 0))
            dve.wait_ge(*at("silu_c", 0))
            for hv in range(4):
                dve.wait_ge(*at("adap", 2 * hv))
                dve.memset(lamt[:, 7:8], 0.0).then_inc(*tick("raw_used", RAW_AT["ada", 2 * hv]))
                dve.wait_ge(*at("adap", 2 * hv + 1))
                dve.tensor_copy(acc[0:2, (hv % 2) * 1024:(hv % 2) * 1024 + 512], PX[0:2, C.noted("bank", ("arow", hv)), :])\
                    .then_inc(*tick("raw_used", RAW_AT["ada", 2 * hv + 1]))
                ada_done(hv)
            split_lo(0)
            split_lo(1)
            for step in PROGRAM:
                if step[0] == "norm":
                    _, n, st, W = step
                    r = rinv_of(n, W)
                    if n not in (0, 7):
                        dve.wait_ge(*at("sd", n))
                        dve.reciprocal(r, r).then_inc(*tick("rinv", n))
                    dve.wait_ge(*at("rinv", n if n != 7 else 6))
                    v = vec_base(st) + (3 if n in (1, 3, 5, 8) else 0)
                    dve.wait_ge(*at("mod", v + 1))
                    for k in range(KD + 1):
                        if k < KD:
                            if k >= 3:
                                dve.wait_ge(*at("hlo", (n, k - 3)))
                            for who in range(W // 256):
                                q = slice(who * 256, who * 256 + 256)
                                ins = dve.scalar_tensor_tensor(out=hslot(k)[:, q], in0=X[:, k * 512 + who * 256:k * 512 + who * 256 + 256],
                                                               scalar=modc(v + 1, who, k), in1=r[:, q], op0=ALU.mult, op1=ALU.mult)
                            ins.then_inc(*tick("xr", (n, k)))
                        if k >= 1:
                            dve.wait_ge(*at("xr", (n, k - 1)))
                            dve.wait_ge(*at("hhi", (n, k - 1)))
                            for who in range(W // 256):
                                o = (k - 1) * W + who * 256
                                ins = dve.scalar_tensor_tensor(out=Hlo[:, o:o + 256], in0=hslot(k - 1)[:, who * 256:who * 256 + 256],
                                                               scalar=modc(v, who, k - 1), in1=Hhi[:, o:o + 256].bitcast(F32),
                                                               op0=ALU.add, op1=ALU.subtract)
                            ins.then_inc(*tick("hlo", (n, k - 1)))
                elif step[0] == "attn":
                    last = UNITS[first_of("out", step[1]) - 1]
                    if is_qk(last):
                        qk_copy(last)
                    attn(step[1])
                elif step[0] == "lsplit":
                    for j in range(NL):
                        dve.wait_ge(*at("hhi", ("x", j)))
                        dve.tensor_tensor(Hlo[:, j * 256:j * 256 + 256], XR[:, j * 256:j * 256 + 256], Hhi[:, j * 256:j * 256 + 256].bitcast(F32),
                                          ALU.subtract).then_inc(*tick("hlo", ("x", j)))
                elif step[0] == "lscan":
                    dve.wait_ge(*at("la", len(GATE_UNITS) - 1))
                    dve.tensor_scalar(XR[:, :], XR[:, :], -1e-30, None, ALU.min).then_inc(*tick("lm", 0))
                    for h in range(2):
                        q = slice(h * 6 * 256, min((h + 1) * 6, NL) * 256)
                        dve.wait_ge(*at("ls", h))
                        link(dve.tensor_tensor(LU[:, q], LU[:, q], XR[:, q], ALU.mult))
                        for j in range(h * 6, min((h + 1) * 6, NL)):
                            q = slice(j * 256, j * 256 + 256)
                            dve.tensor_tensor_scan(XR[:, q], LA[:, q], LU[:, q], 0.0, ALU.mult, ALU.add).then_inc(*tick("lh", j))
                            if j >= 2:
                                scan_lo(j - 2)
                    scan_lo(NL - 2)
                    scan_lo(NL - 1)
                else:
                    u = UNITS[step[1]]
                    i = u["i"]
                    split_lo(i + 2)
                    if u["kind"] in ("up", "down") and UNITS[i - 1]["kind"] == "up":
                        ffn_lo(UNITS[i - 1])
                    evac(u)
                    if i and is_qk(UNITS[i - 1]) and u["kind"] != "out":
                        qk_copy(UNITS[i - 1])
                    if u["kind"] == "bq0":
                        mix(u["st"])
                    for a in ADA_AT[i]:
                        ada(a)
                    for hv in REDUCE_AT[i]:
                        ada_done(hv)

        @block.tensor
        def _(pe):
            items = []
            sums = []

            def take(key):
                n = len(items)
                if n >= AUXN:
                    old = items[n - AUXN]
                    for name in ("aux_act", "aux_dve"):
                        if C.has(name, old):
                            pe.wait_ge(*at(name, old))
                    if old[0] == "arow":
                        pe.wait_ge(*at("raw_used", RAW_AT["ada", 2 * old[1] + 1]))
                items.append(key)
                C.note("bank", key, n % AUXN)
                return PX[:, n % AUXN, :]

            def pm_free(i):
                if i >= 2:
                    u = UNITS[i - 2]
                    for name in ("pm_act", "pm_dve"):
                        if C.has(name, i - 2):
                            pe.wait_ge(*at(name, i - 2))
                    if u["kind"] == "up":
                        pe.wait_ge(*at("cvd", (i - 2, 1)))
                    if u["kind"] == "lin":
                        pe.wait_ge(*at("lxd", u["idx"]))
                    if u["kind"] == "bkv":
                        pe.wait_ge(*at("vcopy", i - 2))
                    if u["kind"] in ("out", "down", "lout", "w2"):
                        n = fed_norm(u)
                        c = chunks_of(u)[-1]
                        if n is not None:
                            pe.wait_ge(*at("xres", (n, c)))
                        elif u["st"] == "M1" and u["kind"] == "w2" and u["idx"] >= KD:
                            pe.wait_ge(*at("xres", ("M1", "last", c)))

            def three(out, st_hi, st_lo, mv_hi, mv_lo, first, last):
                pe.matmul(out, st_hi, mv_hi, start=first, stop=False)
                pe.matmul(out, st_hi, mv_lo, start=False, stop=False)
                return pe.matmul(out, st_lo, mv_hi, start=False, stop=last)

            def operand_ready(u, k):
                kind, st, idx = u["kind"], u["st"], u["idx"]
                if kind in ("cq", "lin", "k", "q") and idx == 0:
                    n = {"L0": 0, "L1": 2, "M0": 4, "KV": 6, "M1": 7}[st]
                    pe.wait_ge(*at("hlo", (n, k)))
                elif kind == "up" and idx == 0:
                    pe.wait_ge(*at("hlo", (1 + 2 * int(st[1]), k)))
                elif kind == "w1" and idx == 0:
                    pe.wait_ge(*at("hlo", (5 if st == "M0" else 8, k)))
                elif kind == "lout" and idx == 0:
                    pe.wait_ge(*at("hlo", ("y", k)))
                elif kind == "down" and idx % KD == 0:
                    pe.wait_ge(*at("glo", u["i"] - HALF + k))
                elif kind == "w2" and idx % KD == 0:
                    if k % 2 == 0:
                        pe.wait_ge(*at("glo", u["i"] - 8 + k // 2))
                elif kind == "out" and idx == 0:
                    if st == "M1":
                        for t in range(2):
                            pe.wait_ge(*at("aux_dve", ("OT", st, ("m", t, k // 4))))
                    elif k < 2:
                        pe.wait_ge(*at("otlo", (st, "a")))
                    elif k < 6:
                        for t in range(NTOK[st]):
                            pe.wait_ge(*at("aux_dve", ("OT", st, ("b", t))))
                    else:
                        for tp in range(NTOK[st] // 2):
                            pe.wait_ge(*at("aux_dve", ("OC", st, tp)))

            def unit(u):
                i, kt, kind = u["i"], u["kt"], u["kind"]
                pe.wait_ge(*at("raw_used", RAW_AT["w", i]))
                pm_free(i)
                mh, ml, S = moving(u)
                if "nt" in u and kind != "au":
                    for t in range(u["nt"]):
                        for k in range(kt):
                            if t == 0:
                                operand_ready(u, k)
                            o = k * S + t * 128
                            ins = three(pm(i, t * 256, 256), mh[:, o:o + 128], ml[:, o:o + 128],
                                        wslot(whi, i, 256, k * 256), wslot(wlo, i, 256, k * 256), k == 0, k == kt - 1)
                elif kind == "lgate":
                    at_ = 0
                    for c, j in enumerate(GATE_UNITS[u["idx"]]):
                        for g in range(2):
                            for m, ci in enumerate(GATES[j]):
                                pe.wait_ge(*at("hlo", ("x", ci)))
                                ins = three(pm(i, c * 512 + g * 256, 256), wslot(whi, i, 128, at_ * 128), wslot(wlo, i, 128, at_ * 128),
                                            mh[:, ci * 256:ci * 256 + 256], ml[:, ci * 256:ci * 256 + 256], m == 0, m == len(GATES[j]) - 1)
                                at_ += 1
                else:
                    W = u["T"]
                    for c in range(u["cols"] // 128):
                        for k in range(kt):
                            if c == 0:
                                operand_ready(u, k)
                            o = k * S
                            w0 = k * u["cols"] + c * 128
                            ins = three(pm(i, c * 512, W), wslot(whi, i, 128, w0), wslot(wlo, i, 128, w0),
                                        mh[:, o:o + W], ml[:, o:o + W], k == 0, k == kt - 1)
                ins.then_inc(*tick("unit", i))

            def transposes(u):
                i, nt = u["i"], u["nt"]
                z = zbuf(u)
                pe.wait_ge(*at("z", i))
                for h in range(len(qk_halves(u))):
                    key = ("qkT", i, h)
                    dst = take(key)
                    for t in range(nt):
                        ins = pe.transpose(dst[:, t * 128:t * 128 + 128], z[:, t * 256 + h * 128:t * 256 + h * 128 + 128], ident)
                    ins.then_inc(*tick("aux", key))

            def ada_sum(hv):
                key = ("ada", hv)
                v = hv // 2
                dst = take(key)
                pe.wait_ge(*at("raw_used", RAW_AT["ada", 2 * hv + 1]))
                for c in range(4):
                    for who in range(2):
                        a = (hv % 2) * 1024 + who * 512 + c * 128
                        if v < CTXV:
                            ins = pe.matmul(dst[:, who * 4 + c:who * 4 + c + 1], acc[:, a:a + 128], ones[:, 0:1], start=True, stop=True)
                        else:
                            ins = pe.matmul(dst[:, c:c + 1], acc[:, a:a + 128], ones[:, 0:1], start=(who == 0), stop=(who == 1))
                ins.then_inc(*tick("aux", key))

            def sumsq(n, k, W):
                if k == 0:
                    if n in (1, 3, 8):
                        st = {1: "L0", 3: "L1", 8: "M1"}[n]
                        g = attention_tiles(st)[-1]["grp"]
                        pe.wait_ge(*at("pm_dve", ("PO", st, g)))
                    elif n:
                        pe.wait_ge(*at("sd", n - 1 if n != 8 else 6))
                pe.wait_ge(*at("sq", (n, k)))
                pe.matmul(PO[:, 0:W], ones, tslot(2 + k % 2, W), start=(k == 0), stop=(k == 7)).then_inc(*tick("sumsq", (n, k)))

            def warm(key):
                dst = take(key)
                for _ in range(WARM_LEN):
                    pe.matmul(dst[:, 0:256], ident, cst[:, 0:256], start=True, stop=True)

            def mix(st):
                pe.wait_ge(*at("mixdma", ("bs", int(st[1]), 1)))
                pe.wait_ge(*at("avn", first_of("av", st)))
                for j in range(2):
                    for tp in range(NTOK[st] // 2):
                        key = ("mix", st, j, tp)
                        dst = take(key)
                        for t in range(2):
                            tt = tp * 2 + t
                            ins = pe.matmul(dst[:, t * 256:t * 256 + 256], vt[:, tt * 640 + j * 128:tt * 640 + j * 128 + 128],
                                            wsT[:, j * 256:j * 256 + 256], start=True, stop=True)
                        ins.then_inc(*tick("aux", key))

            def attn(st):
                tiles = attention_tiles(st)
                Ps, PTs = ptiles(st)
                nt = NTOK[st]
                if st != "M1":
                    pe.wait_ge(*at("pm_act", first_of("cv", st)))
                    pe.wait_ge(*at("pm_act", first_of("au", st)))
                    pe.wait_ge(*at("vcopy", first_of("bkv", st)))
                    pe.wait_ge(*at("aux_dve", ("qkT", first_of("ck", st), 1)))
                    pe.wait_ge(*at("pm_dve", first_of("bkv", st)))
                else:
                    pe.wait_ge(*at("aux_dve", ("qkT", first_of("q", st) + 3, 1)))
                    pe.wait_ge(*at("pm_act", first_of("v", "KV") + 3))
                    pe.wait_ge(*at("pm_dve", first_of("q", st) + 3))
                for n in range(len(tiles) + LO):
                    if n % 4 == 0 and (4 <= n < 64 if st != "M1" else n == 4):
                        warm(("warm", st, n))
                    if n < len(tiles):
                        x = tiles[n]
                        b, K, nk, t = x["base"], x["K"], x["nk"], x["t"]
                        if x["grp"][0] == "b" and x["slot"] == 0:
                            pe.wait_ge(*at("aux_dve", ("qkT", first_of("bkv", st), 0)))
                        if n >= 4:
                            pe.wait_ge(*at("sadd" if st == "M1" else "p", (st, n - 4)))
                        dst = score(n, nk)
                        q, kk, w = (QT, QT, 512) if st != "M1" else (QT2, KT2, 256)
                        mask = x["grp"][0] == "b" and t < 2
                        ins = pe.matmul(dst, q[b:b + K, x["qc"] * w + t * 128:x["qc"] * w + t * 128 + 128],
                                        kk[b:b + K, x["kc"] * w + x["k0"]:x["kc"] * w + x["k0"] + nk], start=True, stop=not mask)
                        if mask:
                            c = 128 * (1 - t)
                            ins = pe.matmul(dst[:, c:c + 128], ident, cst[:, CONST["mask"] + t * 128:CONST["mask"] + t * 128 + 128],
                                            start=False, stop=True)
                        ins.then_inc(*tick("score", (st, n)))
                    m = n - LT
                    if 0 <= m < len(tiles):
                        key = ("T", st, m)
                        dst = take(key)
                        pe.wait_ge(*at("p", (st, m)))
                        for c in range(tiles[m]["nk"] // 128):
                            ins = pe.transpose(dst[:, c * 128:c * 128 + 128], Ps[m % 4][:, c * 128:c * 128 + 128], ident)
                        ins.then_inc(*tick("aux", key))
                    m = n - LP
                    if 0 <= m < len(tiles):
                        x = tiles[m]
                        s = x["slot"]
                        if s == 0:
                            if m == 0:
                                pe.wait_ge(*at("sd", {"L0": 0, "L1": 2, "M1": 6}[st]))
                            else:
                                pe.wait_ge(*at("pm_dve", ("PO", st, tiles[m - 1]["grp"])))
                        pe.wait_ge(*at("aux_dve" if m % 2 else "aux_act", ("T", st, m)))
                        for c, (kt, off) in enumerate(x["v"]):
                            v = vt[:, kt * 640 + off:kt * 640 + off + 64] if st != "M1" else VT2[:, kt * 1024 + off:kt * 1024 + off + 64]
                            ins = pe.matmul(PO[:, s * 64:s * 64 + 64], PTs[m % 4][:, c * 128:c * 128 + 128], v,
                                            start=(c == 0), stop=(c == len(x["v"]) - 1))
                        ins.then_inc(*tick("pv", (st, m)))
                    m = n - LO
                    if m >= 0 and tiles[m]["slot"] == 7 and tiles[m]["grp"][0] != "c":
                        x = tiles[m]
                        key = ("OT", st, x["grp"])
                        dst = take(key)
                        g = groups[st, x["grp"]]
                        pe.wait_ge(*at("pm_dve", ("PO", st, x["grp"])))
                        for c in range(4):
                            ins = pe.transpose(dst[:, c * 128:c * 128 + 128], tslot(g % 2)[:, c * 128:c * 128 + 128], ident)
                        ins.then_inc(*tick("aux", key))
                    if st != "M1" and n == last_c(st) + LO:
                        pe.wait_ge(*at("ocn", st))
                        for tp in range(nt // 2):
                            key = ("OC", st, tp)
                            dst = take(key)
                            for c in range(2):
                                for t in range(2):
                                    o = 1024 + (tp * 2 + t) * 256 + c * 128
                                    ins = pe.transpose(dst[:, c * 256 + t * 128:c * 256 + t * 128 + 128], T[:, o:o + 128], ident)
                            ins.then_inc(*tick("aux", key))

            pe.wait_ge(*at("cstdma", 0))
            for k in range(KD):
                sumsq(0, k, 512)
            pe.wait_ge(*at("silu_c", 0))
            for hv in range(4):
                key = ("arow", hv)
                dst = take(key)
                for part in range(2):
                    n = RAW_AT["ada", 2 * hv + part]
                    raw_ready(pe, ("ada", 2 * hv + part))
                    for k in range(4):
                        kk = part * 4 + k
                        ins = pe.matmul(dst[0:2, :], silc[:, kk:16:8], slot_raw(n, UMAX)[:, k * 512:k * 512 + 512],
                                        start=(kk == 0), stop=(kk == 7))
                    ins.then_inc(*tick("adap", 2 * hv + part))
                key = ("ada", hv)
                dst = take(key)
                pe.wait_ge(*at("raw_used", RAW_AT["ada", 2 * hv + 1]))
                for c in range(4):
                    a = (hv % 2) * 1024 + c * 128
                    ins = pe.transpose(dst[:, 2 * c:2 * c + 2], acc[0:2, a:a + 128], ident[0:2, 0:2])
                ins.then_inc(*tick("aux", key))
            late = []
            for step in PROGRAM:
                if step[0] in ("norm", "attn"):
                    for a in late:
                        sumsq(*a)
                    late = []
                if step[0] == "attn":
                    last = UNITS[first_of("out", step[1]) - 1]
                    if is_qk(last):
                        transposes(last)
                    attn(step[1])
                if step[0] == "unit":
                    u = UNITS[step[1]]
                    i = u["i"]
                    unit(u)
                    for a in late:
                        sumsq(*a)
                    late = []
                    if i and is_qk(UNITS[i - 1]) and u["kind"] != "out":
                        transposes(UNITS[i - 1])
                    if u["kind"] == "bq0":
                        mix(u["st"])
                    for hv in REDUCE_AT[i]:
                        ada_sum(hv)
                    n = fed_norm(u)
                    if n is not None:
                        late = [(n, k, 512 if u["st"] == "L0" or n == 2 else 256) for k in chunks_of(u)]
        return C.seen


def _units_of(w, kt, order=None):
    K, N = w.shape
    out = []
    for cols in order:
        part = w[:, cols]
        for a in range(0, K // P, kt):
            blk = part[a * P:(a + kt) * P].reshape(kt, P, len(cols))
            out.append(blk.transpose(1, 0, 2).reshape(P, kt * len(cols)))
    return out


def _lay_out(I):
    f = {k: np.asarray(v) for k, v in I.items()}
    ar = np.arange
    group = lambda n, w: [ar(a, a + w) for a in range(0, n, w)]
    store = {}
    place = [None] * NU
    hb = np.concatenate([ar(h * 64, h * 64 + 64) for h in HEADS_B])

    def put(i, a):
        u = UNITS[i]
        name = {"L": "wl", "M": "wm", "K": "wm"}[u["st"][0]] + f"_{a.shape[1]}"
        place[i] = len(store.setdefault(name, []))
        store[name].append(a)

    pos = 0
    for l in range(2):
        w = f["w_in"][l]
        order = [ar(1280, 1536), ar(1536, 1792), ar(256, 512), ar(0, 256), 512 + hb[:256], 512 + hb[256:], ar(1024, 1280), ar(1792, 2048)]
        seq = _units_of(w, KD, order)
        wo = f["w_out"][l][np.concatenate([ar(256), 256 + hb, ar(768, 1024)])]
        seq += _units_of(wo, KD, group(D, 256))
        for h in range(2):
            seq += _units_of(f["w_up"][l], KD, [np.concatenate([ar(j * P, j * P + P), FF + ar(j * P, j * P + P)])
                                               for j in range(h * HALF, (h + 1) * HALF)])
            seq += _units_of(f["w_down"][l][h * HALF * P:(h + 1) * HALF * P], HALF, group(D, 128))
        for a in seq:
            put(pos, a)
            pos += 1
    seq = _units_of(f["lru_w_in_2"][0], KD, [np.concatenate([ar(j * P, j * P + P), LW + ar(j * P, j * P + P)]) for j in range(NL)])
    dense = []
    for name in ("lru_gate_a_w_2", "lru_gate_x_w_2"):
        m = np.zeros((LW, LW), np.float32)
        for b in range(LW // LB):
            m[b * LB:(b + 1) * LB, b * LB:(b + 1) * LB] = f[name][0, b]
        dense.append(m)
    for js in GATE_UNITS:
        seq.append(np.concatenate([dense[g][m * P:(m + 1) * P, j * P:(j + 1) * P] for j in js for g in range(2) for m in GATES[j]], axis=1))
    seq += _units_of(f["lru_w_out_2"][0], NL, group(D, 128))

    def mlp(l):
        out = []
        for h in range(2):
            out += _units_of(f["mlp_w1_2"][l], KD, [ar(h * 2048 + a, h * 2048 + a + 256) for a in range(0, 2048, 256)])
            out += _units_of(f["mlp_w2_2"][l][h * 2048:(h + 1) * 2048], 16, group(D, 128))
        return out

    seq += mlp(0) + _units_of(f["kv_w_2"], KD, group(2 * D, 256))
    seq += _units_of(f["attn_w_q_2"][0], KD, group(D, 256)) + _units_of(f["attn_w_o_2"][0], KD, group(D, 256)) + mlp(1)
    for a in seq:
        put(pos, a)
        pos += 1
    assert pos == NU
    ada, bada = [], []
    for w, b in ((f["w_ada"][0], f["b_ada"][0]), (f["w_ada"][1], f["b_ada"][1]), (f["ada_w_2"][0], f["ada_b_2"][0]),
                 (f["kv_ada_w_2"], f["kv_ada_b_2"]), (f["ada_w_2"][1], f["ada_b_2"][1])):
        ada += _units_of(w, 4, group(w.shape[1], 512))
        bada.append(b)
    col = lambda v: np.asarray(v).reshape(-1, P).T
    feat = np.concatenate(
        [col(np.concatenate(bada))]
        + [col(g) for g in (f["norm1_g"][0], f["norm2_g"][0], f["norm1_g"][1], f["norm2_g"][1], f["norm1_g_2"][0], f["norm2_g_2"][0],
                            f["kv_norm_g_2"], f["norm1_g_2"][1], f["norm2_g_2"][1])]
        + [col(f["conv_w"][:, :, 0, :]), col(f["conv_b"]), col(f["lru_conv_w_2"][0]), col(f["lru_conv_b_2"][0]),
           col(f["lru_gate_a_b_2"][0]), col(f["lru_gate_x_b_2"][0]), col(f["lru_lambda_2"][0]), col(f["c"]), col(f["c_ctx"]), col(f["c_2"])], axis=1)
    assert feat.shape[1] == NFEAT
    rows = []
    for l in range(2):
        rows += [f["b_qnorm"][l], f["b_knorm"][l], f["c_qnorm"][l], f["c_knorm"][l], f["c_lam"][l].ravel(), f["c_subln"][l], f["b_sink"][l][HEADS_B]]
    rows = np.concatenate(rows + [f["k_norm_g_2"], f["q_norm_g_2"][0]])
    assert rows.shape[0] == NROW
    x0 = np.concatenate([f["x"][0], f["ctx"][0]]).T.reshape(KD, P, 512).transpose(1, 0, 2).reshape(P, KD * 512)
    wsT = f["a_ws"].transpose(0, 3, 1, 2).reshape(2, P, 512)
    abs_ = f["a_bs"].reshape(2, 2, 2, P).transpose(0, 2, 1, 3).reshape(2, 2, 256)
    q, k = ar(128)[:, None] + 128, ar(256)[None, :]
    bias = f["rel_bias_2"][0][:, np.clip(q - k, -128, 128) + 128].transpose(1, 0, 2)
    out = {n: np.stack(v) for n, v in store.items()}
    out.update(ada=np.stack(ada), feat=feat, rows=rows, x0=x0, wsT=wsT, abs=abs_, bias=bias, cst=_constants())
    return {n: np.ascontiguousarray(v, np.float32) for n, v in out.items()}, place


def _constants():
    c = np.zeros((P, NCONST), np.float32)
    c[:, 0:128] = np.eye(P)
    c[:, 128:256] = 1.0
    p, j = np.arange(P)[:, None], np.arange(P)[None, :]
    c[:, 256:384] = np.where(j <= p, 0.0, NEG)
    c[:, 384:512] = np.where(j >= p, 0.0, NEG)
    tok = np.arange(SEQ)
    pos = np.stack([tok // 64, tok % 64], 1).astype(np.float32)
    for d, a, b in ((64, CONST["cb"], CONST["sb"]), (32, CONST["cc"], CONST["sc"])):
        f = d // 4
        inv = np.float32(10000.0) ** (-np.arange(f, dtype=np.float32) / np.float32(f))
        ang = (pos[:, :, None] * inv.astype(np.float32)).astype(np.float32)
        cos, sin = np.cos(ang), np.sin(ang)
        cs = np.stack([cos, cos], 2).reshape(2, P, d).transpose(1, 0, 2).reshape(P, 2 * d)
        sn = np.stack([-sin, sin], 2).reshape(2, P, d).transpose(1, 0, 2).reshape(P, 2 * d)
        c[:, a:a + 2 * d] = cs
        c[:, b:b + 2 * d] = sn
    return c


def write_program(nc, arrays, place, known):
    A = {n: nc.dram_tensor(f"in_{n}", a.shape, F32, kind="ExternalInput").ap() for n, a in arrays.items()}
    A["out"] = nc.dram_tensor("out_x", (P, KD, SEQ), F32, kind="ExternalOutput").ap()
    A["place"] = place
    return build(nc, A, known)


def kernel(**inputs):
    import concourse.bacc as bacc
    from concourse.bass_utils import run_bass_kernel_spmd
    arrays, place = _lay_out(inputs)
    counts = {}
    for _ in range(2):
        nc = bacc.Bacc("TRN2", target_bir_lowering=False, num_devices=1)
        counts = write_program(nc, arrays, place, counts)
    r = run_bass_kernel_spmd(nc, [{f"in_{n}": a for n, a in arrays.items()}], core_ids=[0])
    got = r.results[0]["out_x"]
    return np.ascontiguousarray(got.transpose(2, 1, 0).reshape(1, SEQ, D))
```
